# Optimizing a Trainium2 kernel written in Bass

```python
import math
import jax, jax.numpy as jnp
from jax import lax
import numpy as np

D_MODEL = 1024
BATCH = 1
SEQ = 1024
DEPTH = 1

D_POOL = D_MODEL
POOL_WINDOWS = (2, 4, 8, 16)
POOL_GROUPS = len(POOL_WINDOWS)
POOL_GROUP_WIDTH = D_POOL // POOL_GROUPS
D_SSM = D_MODEL
SSM_GROUP = 16
SSM_GROUPS = D_SSM // SSM_GROUP
SSM_STATE = 64
DT_MIN = 1e-3
DT_MAX = 1e-1
RMS_EPS = 1e-6
IN_SPLITS = (D_POOL, 2 * D_POOL, 2 * D_POOL + D_SSM, 2 * D_POOL + 2 * D_SSM,
             2 * D_POOL + 2 * D_SSM + D_MODEL)
IN_COLS = 2 * D_POOL + 2 * D_SSM + 2 * D_MODEL

kernel_name = 'hybrid_pool_s5_gated_block'

def rmsnorm(x, gain):
    xf = x.astype(jnp.float32)
    y = xf * lax.rsqrt(jnp.mean(xf * xf, axis=-1, keepdims=True) + RMS_EPS)
    return (y * gain.astype(jnp.float32)).astype(x.dtype)

def causal_pool_mixer(u, pool_w, pool_scale):
    bsz, seq, _ = u.shape
    uf = u.astype(jnp.float32)
    csum = jnp.cumsum(uf, axis=1)
    pos = jnp.arange(1, seq + 1, dtype=jnp.float32)[None, :, None]
    pooled = []
    for g, w in enumerate(POOL_WINDOWS):
        cs = csum[..., g * POOL_GROUP_WIDTH:(g + 1) * POOL_GROUP_WIDTH]
        lagged = jnp.pad(cs, ((0, 0), (w, 0), (0, 0)))[:, :seq]
        count = jnp.minimum(pos, float(w))
        pooled.append((cs - lagged) / count)
    pooled = (jnp.concatenate(pooled, axis=-1) - uf).astype(u.dtype)
    pooled = pooled.reshape(bsz, seq, POOL_GROUPS, POOL_GROUP_WIDTH)
    mixed = jnp.einsum('blgc,gcd->blgd', pooled, pool_w).reshape(bsz, seq, D_POOL)
    return mixed * pool_scale

def _complex_linear_combine(e1, e2):
    ar1, ai1, br1, bi1 = e1
    ar2, ai2, br2, bi2 = e2
    ar = ar2 * ar1 - ai2 * ai1
    ai = ar2 * ai1 + ai2 * ar1
    br = ar2 * br1 - ai2 * bi1 + br2
    bi = ar2 * bi1 + ai2 * br1 + bi2
    return (ar, ai, br, bi)

def s5_mixer(u, a_re, a_im, log_dt, b_re, b_im, c_re, c_im, d_skip, glu_w, glu_b):
    bsz, seq, _ = u.shape
    uf = u.astype(jnp.float32).reshape(bsz, seq, SSM_GROUPS, SSM_GROUP)
    dt = jnp.exp(log_dt.astype(jnp.float32))[:, None]
    lam_re = jnp.minimum(a_re.astype(jnp.float32), -1e-4)
    lam_im = a_im.astype(jnp.float32)
    mag = jnp.exp(lam_re * dt)
    abar_re = mag * jnp.cos(lam_im * dt)
    abar_im = mag * jnp.sin(lam_im * dt)
    den = lam_re * lam_re + lam_im * lam_im
    num_re = abar_re - 1.0
    f_re = (num_re * lam_re + abar_im * lam_im) / den
    f_im = (abar_im * lam_re - num_re * lam_im) / den
    f_re, f_im = f_re[:, :, None], f_im[:, :, None]
    bb_re = f_re * b_re - f_im * b_im
    bb_im = f_re * b_im + f_im * b_re
    bu_re = jnp.einsum('blgh,gph->blgp', uf, bb_re)
    bu_im = jnp.einsum('blgh,gph->blgp', uf, bb_im)
    a_seq_re = jnp.broadcast_to(abar_re[None, None], (1, seq, SSM_GROUPS, SSM_STATE))
    a_seq_im = jnp.broadcast_to(abar_im[None, None], (1, seq, SSM_GROUPS, SSM_STATE))
    _, _, s_re, s_im = lax.associative_scan(
        _complex_linear_combine, (a_seq_re, a_seq_im, bu_re, bu_im), axis=1)
    y = (jnp.einsum('blgp,ghp->blgh', s_re, c_re)
         - jnp.einsum('blgp,ghp->blgh', s_im, c_im)
         + d_skip * uf)
    y = jax.nn.gelu(y.reshape(bsz, seq, D_SSM).astype(u.dtype))
    return y * jax.nn.sigmoid(y @ glu_w + glu_b)

def hybrid_layer(x, c, w_ada, b_ada, norm_pre, norm_post, w_in, pool_w, pool_scale,
                 a_re, a_im, log_dt, b_re, b_im, c_re, c_im, d_skip, glu_w, glu_b,
                 w_branch_pool, w_branch_ssm, w_out):
    mod = jax.nn.silu(c) @ w_ada + b_ada
    shift, scale, gate = jnp.split(mod, 3, axis=-1)
    h = rmsnorm(x, norm_pre) * (1.0 + scale[:, None, :]) + shift[:, None, :]
    proj = h @ w_in
    u_pool, z_pool, u_ssm, z_ssm, g_pool, g_ssm = jnp.split(proj, list(IN_SPLITS), axis=-1)
    y_pool = causal_pool_mixer(u_pool, pool_w, pool_scale) * jax.nn.silu(z_pool)
    y_ssm = s5_mixer(u_ssm, a_re, a_im, log_dt, b_re, b_im, c_re, c_im, d_skip,
                     glu_w, glu_b) * jax.nn.silu(z_ssm)
    merged = (jax.nn.sigmoid(g_pool) * (y_pool @ w_branch_pool)
              + jax.nn.sigmoid(g_ssm) * (y_ssm @ w_branch_ssm))
    out = merged @ w_out
    return x + gate[:, None, :] * rmsnorm(out, norm_post)

def setup_inputs(seed: int = 0) -> dict:
    key = jax.random.key(seed)
    ks = jax.random.split(key, 24)
    f32 = jnp.float32

    def nrm(k, shape, s):
        return jax.random.normal(k, shape, f32) * s

    G, P, H = SSM_GROUPS, SSM_STATE, SSM_GROUP
    n_idx = jnp.arange(P, dtype=f32)
    return {
        'x': nrm(ks[0], (BATCH, SEQ, D_MODEL), 1.0),
        'c': nrm(ks[1], (BATCH, D_MODEL), 1.0),
        'w_ada': nrm(ks[2], (DEPTH, D_MODEL, 3 * D_MODEL), 0.5 * D_MODEL ** -0.5),
        'b_ada': nrm(ks[3], (DEPTH, 3 * D_MODEL), 0.02),
        'norm_pre': 1.0 + nrm(ks[4], (DEPTH, D_MODEL), 0.02),
        'norm_post': 1.0 + nrm(ks[5], (DEPTH, D_MODEL), 0.02),
        'w_in': nrm(ks[6], (DEPTH, D_MODEL, IN_COLS), D_MODEL ** -0.5),
        'pool_w': nrm(ks[7], (DEPTH, POOL_GROUPS, POOL_GROUP_WIDTH, POOL_GROUP_WIDTH),
                      POOL_GROUP_WIDTH ** -0.5),
        'pool_scale': 1.0 + nrm(ks[8], (DEPTH, D_POOL), 0.02),
        'ssm_a_re': -0.5 + nrm(ks[9], (DEPTH, G, P), 0.01),
        'ssm_a_im': math.pi * n_idx + nrm(ks[10], (DEPTH, G, P), 0.01),
        'ssm_log_dt': jax.random.uniform(ks[11], (DEPTH, G), f32,
                                         math.log(DT_MIN), math.log(DT_MAX)),
        'ssm_b_re': nrm(ks[12], (DEPTH, G, P, H), (2 * H) ** -0.5),
        'ssm_b_im': nrm(ks[13], (DEPTH, G, P, H), (2 * H) ** -0.5),
        'ssm_c_re': nrm(ks[14], (DEPTH, G, H, P), P ** -0.5),
        'ssm_c_im': nrm(ks[15], (DEPTH, G, H, P), P ** -0.5),
        'ssm_d': nrm(ks[16], (DEPTH, G, H), 0.5),
        'glu_w': nrm(ks[17], (DEPTH, D_SSM, D_SSM), D_SSM ** -0.5),
        'glu_b': nrm(ks[18], (DEPTH, D_SSM), 0.02),
        'w_branch_pool': nrm(ks[19], (DEPTH, D_POOL, D_MODEL), D_POOL ** -0.5),
        'w_branch_ssm': nrm(ks[20], (DEPTH, D_SSM, D_MODEL), D_SSM ** -0.5),
        'w_out': nrm(ks[21], (DEPTH, D_MODEL, D_MODEL), D_MODEL ** -0.5),
    }

def reference(x, c, w_ada, b_ada, norm_pre, norm_post, w_in, pool_w, pool_scale,
              ssm_a_re, ssm_a_im, ssm_log_dt, ssm_b_re, ssm_b_im, ssm_c_re, ssm_c_im,
              ssm_d, glu_w, glu_b, w_branch_pool, w_branch_ssm, w_out):
    for layer in range(DEPTH):
        x = hybrid_layer(x, c, w_ada[layer], b_ada[layer], norm_pre[layer], norm_post[layer],
                         w_in[layer], pool_w[layer], pool_scale[layer],
                         ssm_a_re[layer], ssm_a_im[layer], ssm_log_dt[layer],
                         ssm_b_re[layer], ssm_b_im[layer], ssm_c_re[layer], ssm_c_im[layer],
                         ssm_d[layer], glu_w[layer], glu_b[layer],
                         w_branch_pool[layer], w_branch_ssm[layer], w_out[layer])
    return x


_drawn_inputs = setup_inputs


def setup_inputs(seed=0):
    import zlib

    import numpy as np

    out = dict(_drawn_inputs(seed))
    spreads = {}
    factors = {'norm_pre': 6.655,
     'norm_post': 22.46,
     'pool_scale': 25.821,
     'ssm_a_re': 64.0,
     'ssm_a_im': 43.256,
     'ssm_log_dt': 50.68,
     'ssm_b_re': 61.04,
     'ssm_b_im': 61.2,
     'ssm_c_re': 59.496,
     'ssm_c_im': 61.12,
     'glu_w': 6.216,
     'glu_b': 64.0}
    for name, (base, spread) in spreads.items():
        noise = np.random.default_rng([zlib.crc32(name.encode()), seed]).standard_normal(out[name].shape)
        drawn = base * np.exp(spread * noise) if base else spread * noise
        out[name] = __import__('jax').numpy.asarray(drawn.astype(out[name].dtype))
    for name, factor in factors.items():
        out[name] = (out[name] * factor).astype(out[name].dtype)
    return out
```

```python
from contextlib import ExitStack
import concourse.bass as bass
from concourse import mybir
from concourse.alu_op_type import AluOpType as ALU

ACT = mybir.ActivationFunctionType
F32 = mybir.dt.float32
F32R = mybir.dt.float32r
I32 = mybir.dt.int32

P = 128
D = 1024
KT = D // P
SEQ = 1024
CH = 8
NC = SEQ // CH
HALF = 512
G = 64
SG = 16
NS = 64
GB = P // SG
WINDOWS = (2, 4, 8, 16)
LEVELS = 4
EPS = 1e-6
CF = 96
TILE = 4096

J_POOL, W_POOL = 8, 0
J_F1, W_F1 = 40, 32
J_BP, W_BP = 42, 34
J_F2, W_F2 = 58, 58
J_GLU, W_GLU = 60, 60
J_F3, W_F3 = 76, 76
J_BS, W_BS = 80, 80
J_OUT = 88
W_ALL = 88


def half_pi_parts():
    unit = 10 ** 35
    rest, parts = 157079632679489661923132169163975144, []
    rest <<= 34
    for bits in (10, 22, 34):
        n = rest // (unit << (34 - bits))
        parts.append(n / 2 ** bits)
        rest -= n * (unit << (34 - bits))
    return parts + [rest / (unit << 34)]


class Steps:

    def __init__(self, eng, sem):
        self.eng, self.sem, self.base, self.k, self.turn, self.per = eng, sem, 0, 0, None, 0

    def did(self, ins):
        ins.then_inc(self.sem, 1)
        self.k += 1

    def landed(self):
        v = self.base + self.k
        self.eng.wait_ge(self.sem, v if self.turn is None else self.turn * self.per + v)

    def do(self, ins):
        self.did(ins)
        self.landed()

    def loop(self, turn, per):
        self.base, self.k, self.turn, self.per = self.base + self.k, 0, turn, per

    def end(self, turns):
        assert self.k == self.per, (self.k, self.per)
        self.base, self.k, self.turn = self.base + self.per * turns, 0, None


def build(nc, x, cols_d, consts_d, a_re_d, a_im_d, log_dt_d, bc_d, w_ada_d, wstream_d, w_out_d, out):
    ctx = ExitStack()
    with ctx:
        def sem(name):
            return ctx.enter_context(nc.semaphore(name))

        def psum(name):
            return ctx.enter_context(nc.psum_tensor(name, [P, 2 * HALF], F32))

        cur = [-(-nc.sbuf_base // 64) * 64]

        def at(name, shape, offset, dt=F32):
            return nc.alloc_sbuf_tensor_at(name, shape, dt, offset=offset)

        def nbytes(shape):
            n = 4
            for s in shape[1:]:
                n *= s
            return -(-n // 32) * 32

        def new(name, shape, dt=F32):
            t = at(name, shape, cur[0], dt)
            cur[0] += nbytes(shape)
            return t

        big = [P, KT, SEQ]
        h_hi_at = cur[0]
        h_hi = new("h_hi", big, F32R)
        h_lo = new("h_lo", big, F32R)
        ada = at("ada", [P, 2 * KT, KT, P], h_hi_at)
        m_hi = at("m_hi", big, h_hi_at, F32R)
        m_lo = at("m_lo", big, h_hi_at + 8 * TILE, F32R)
        raw_at = cur[0]
        raw = [new(f"raw{s}", [P, KT, P]) for s in range(2)]
        w_hi = [new(f"w_hi{s}", [P, KT, P], F32R) for s in range(2)]
        w_lo = [new(f"w_lo{s}", [P, KT, P], F32R) for s in range(2)]
        squares = at("squares", [P, SEQ], raw_at)
        gt = [new(f"gt{s}", [P, SEQ]) for s in range(2)]
        rt = [new(f"rt{s}", [P, SEQ]) for s in range(2)]
        a_at = cur[0]
        b_at, c_at = a_at + 8 * TILE, a_at + 16 * TILE
        cur[0] = a_at + 24 * TILE

        x_tok = at("x_tok", big, a_at)
        coef = at("coef", [P, G, CF], c_at)
        in_hi = at("in_hi", big, a_at, F32R)
        in_raw = at("in_raw", big, c_at)
        in_lo = at("in_lo", big, c_at, F32R)
        ys_raw = at("ys_raw", big, b_at)
        ys_lo = at("ys_lo", big, b_at, F32R)
        wo_raw = at("wo_raw", [P, KT, D], c_at)
        wo_lo = at("wo_lo", [P, KT, D], c_at, F32R)
        wo_hi = at("wo_hi", [P, KT, D], a_at, F32R)

        p1 = [a_at]

        def ssm(name, shape, dt=F32):
            t = at(name, shape, p1[0], dt)
            p1[0] += nbytes(shape)
            return t

        cf = ssm("cf", [P, GB, CF])
        bc = ssm("bc", [P, 5, GB, SG])
        v = ssm("v", [P, GB, CH, SG])
        vt = ssm("vt", [P, GB, CH, SG])
        wout = ssm("wout", [P, GB, CH, SG])
        cc = ssm("cc", [P, GB, SG])
        cos_t = ssm("cos_t", [P, GB, NC])
        sin_t = ssm("sin_t", [P, GB, NC])
        win = ssm("win", [P, GB, P])
        ks = ssm("ks", [P, GB, SG])
        dk = ssm("dk", [P, GB, SG])
        toep = ssm("toep", [P, CH, GB, SG])
        taps = ssm("taps", [P, GB, CH, SG])
        u_in = ssm("u_in", [P, GB, NC])
        u_out = ssm("u_out", [P, SEQ])
        st = ssm("st", [P, GB, NC])
        sw = ssm("sw", [P, GB, NC])
        sq = ssm("sq", [P, GB, NC])
        y_act = ssm("y_act", [P, GB, NC])
        pad = [P, CH, NC + 1]
        pu, pa, pb = ssm("pu", pad), ssm("pa", pad), ssm("pb", pad)
        pfix = ssm("pfix", [P, CH, 2])
        pool_hi = ssm("pool_hi", [P, 2, SEQ], F32R)
        pool_lo = ssm("pool_lo", [P, 2, SEQ], F32R)
        assert p1[0] <= cur[0], (p1[0], cur[0])

        cols = new("cols", [P, 64])
        consts = new("consts", [P, 232])
        silu_c = new("silu_c", [P, KT])
        g_col = new("g_col", [P, KT])
        s_col = new("s_col", [P, KT])
        gate_col = new("gate_col", [P, KT])
        glub = new("glub", [P, KT])
        r8 = new("r8", [P, KT, GB])
        stat = new("stat", [P, 6, 8])
        gate_row = new("gate_row", [P, D])
        ones = new("ones", [P, P])
        assert cur[0] <= nc.sbuf_usable_end, cur[0]

        c_in, npre, b_ada = cols[:, 0:8], cols[:, 8:16], cols[:, 16:40]
        npost, pscale, glu_b = cols[:, 40:48], cols[:, 48:56], cols[:, 56:64]
        ident = consts[:, 0:128]
        sign = consts[:, 128:129]
        level_on = consts[:, 129:145].rearrange("p (g l) -> p g l", l=LEVELS)
        inv_w = consts[:, 145:149]
        inv_n = consts[:, 149:213].rearrange("p (g t c) -> p g t c", t=CH, c=2)
        dmask = consts[:, 213:229]

        ps = [psum("ps0"), psum("ps1")]
        psa = psum("psa")
        psb = psum("psb")

        def scratch(name, shape):
            return nc.dram_tensor(name, shape, F32).ap()

        coef_d = scratch("coef_d", [KT, P, GB * CF])
        k_d = scratch("k_d", [KT, P, GB * SG])
        u_d = scratch("u_d", [KT, P, SEQ])
        y_d = scratch("y_d", [KT, P, SEQ])
        yp_d = scratch("yp_d", [KT, P, SEQ])
        m1_d = scratch("m1_d", [KT, P, SEQ])
        gs_d = scratch("gs_d", [KT, P, SEQ])

        small_in = sem("small_in")
        ada_in = [sem(f"ada_in{q}") for q in range(4)]
        tile_in = [sem(f"tile_in{n}") for n in range(KT)]
        raw_in = [sem("raw_in0"), sem("raw_in1")]
        raw_free = [sem("raw_free0"), sem("raw_free1")]
        hi_done, mm_done = sem("hi_done"), sem("mm_done")
        job_out = [sem("job_out0"), sem("job_out1")]
        silu_c_ready, mod_done, mod_ready = sem("silu_c_ready"), sem("mod_done"), sem("mod_ready")
        x_sums, x_var, x_root, x_scaled = sem("x_sums"), sem("x_var"), sem("x_root"), sem("x_scaled")
        h_done = sem("h_done")
        dve_step, pool_step = sem("dve_step"), sem("pool_step")
        coef_ready, coef_stored, coef_in = sem("coef_ready"), sem("coef_stored"), sem("coef_in")
        pads_ready = sem("pads_ready")
        v_ready, tables_ready, wout_ready = sem("v_ready"), sem("tables_ready"), sem("wout_ready")
        a_done, win_ready, k_taken, k_ready = sem("a_done"), sem("win_ready"), sem("k_taken"), sem("k_ready")
        k_stored, toep_in, taps_ready = sem("k_stored"), sem("toep_in"), sem("taps_ready")
        u_stored, u_loaded = sem("u_stored"), sem("u_loaded")
        x_done, swapped, x_taken = sem("x_done"), sem("swapped"), sem("x_taken")
        z_ready, tables_used, sq_ready = sem("z_ready"), sem("tables_used"), sem("sq_ready")
        y_done, y_taken, y_stored = sem("y_done"), sem("y_taken"), sem("y_stored")
        pooled, pool_hi_done, pool_lo_done = sem("pooled"), sem("pool_hi_done"), sem("pool_lo_done")
        yp_stored = [sem("yp_stored0"), sem("yp_stored1")]
        gs_stored = [sem("gs_stored0"), sem("gs_stored1")]
        m1_stored = [sem("m1_stored0"), sem("m1_stored1")]
        in_hi_done, in_lo_done = sem("in_hi_done"), sem("in_lo_done")
        gate_taken, diag_ready, row_done, row_ready = (sem("gate_taken"), sem("diag_ready"),
                                                       sem("row_done"), sem("row_ready"))
        reload_in = [sem("reload_in0"), sem("reload_in1")]
        gated = sem("gated")
        g_in = [sem("g_in0"), sem("g_in1")]
        m_sum, m_hi_done, m_lo_done = sem("m_sum"), sem("m_hi_done"), sem("m_lo_done")
        o_sums, o_var, o_root, o_ready = sem("o_sums"), sem("o_var"), sem("o_root"), sem("o_ready")
        out_stored = [sem("out_stored0"), sem("out_stored1")]

        block = ctx.enter_context(nc.Block())

        def half(base, per, i, k):
            return base // 2 + k // 2 + (per // 2) * i

        x_view = x.rearrange("o (c t) d -> (o t) c d", t=CH)
        o_view = out.rearrange("o (c t) d -> (o t) c d", t=CH)

        def newton(steps, cols_, factor):
            tt, stt, ts = nc.vector.tensor_tensor, nc.vector.scalar_tensor_tensor, nc.vector.tensor_scalar
            var, root, r, t = stat[:, 1, cols_], stat[:, 2, cols_], stat[:, 3, cols_], stat[:, 4, cols_]
            steps.do(nc.vector.reciprocal(r, root))
            steps.do(tt(t, r, r, ALU.mult))
            steps.do(stt(t, t, -0.5, var, ALU.mult, ALU.mult))
            steps.do(stt(t, t, 1.5, r, ALU.add, ALU.mult))
            if factor != 1.0:
                steps.do(ts(t, t, factor, None, ALU.mult))

        names = ["are", "aim", "ldt", "dt", "f_re", "f_im", "den", "num", "t1", "t2", "t3", "t4"]
        par, off = {}, b_at
        for nme in names:
            par[nme] = at("par_" + nme, [P, G], off)[:, :]
            off += 4 * G
        wide = {}
        for nme in ["arg", "k", "r", "p", "q", "mag", "ang", "sn", "cs", "z", "cw", "sw2"]:
            wide[nme] = at("par_w_" + nme, [P, 2 * G], off)[:, :]
            off += 8 * G
        bits = at("par_bits", [P, 2 * G], off, I32)
        off += 8 * G
        pw_re, pw_im = at("pw_re", [P, G, 9], off), at("pw_im", [P, G, 9], off + 36 * G)
        off += 72 * G
        tmp_a, tmp_b = at("tmp_a", [P, G, 8], off), at("tmp_b", [P, G, 8], off + 32 * G)
        off += 64 * G
        e_re, e_im = at("e_re", [P, 7, G], off), at("e_im", [P, 7, G], off + 28 * G)
        off += 56 * G
        assert off <= c_at

        def coefficients(dve, steps):
            do = steps.do
            tt, stt, ts = nc.vector.tensor_tensor, nc.vector.scalar_tensor_tensor, nc.vector.tensor_scalar
            MAGIC = 12582912.0

            def rounded(out_, in_, scale):
                do(ts(out_, in_, scale, None, ALU.mult))
                do(ts(out_, out_, MAGIC, None, ALU.add))
                do(ts(out_, out_, MAGIC, None, ALU.subtract))

            def exp(out_, in_, width):
                k, r, p, q = (wide[z][:, 0:width] for z in ("k", "r", "p", "q"))
                do(ts(q, in_, -87.0, 88.0, ALU.max, ALU.min))
                rounded(k, q, 1.4426950408889634)
                do(stt(r, k, -0.693359375, q, ALU.mult, ALU.add))
                do(stt(r, k, 2.12194440054690583e-4, r, ALU.mult, ALU.add))
                c = [1.0, 1 / 2, 1 / 6, 1 / 24, 1 / 120, 1 / 720]
                do(ts(p, r, 1 / 5040, None, ALU.mult))
                for a in reversed(c):
                    do(stt(p, p, a, r, ALU.add, ALU.mult))
                do(ts(p, p, 1.0, None, ALU.add))
                do(ts(bits[:, 0:width], k, 127.0, 8388608.0, ALU.add, ALU.mult))
                do(tt(p, p, bits[:, 0:width].bitcast(F32), ALU.mult))
                do(stt(out_, in_, -87.0, p, ALU.is_ge, ALU.mult))

            def cos_sin(cs, sn, ang):
                k, r, p, q, z = (wide[m] for m in ("k", "r", "p", "q", "z"))
                parts = half_pi_parts()
                src = ang
                for scale in (2048.0, 1.0):
                    rounded(k, src, 1.0 / (1.5707963267948966 * scale))
                    for part in parts:
                        do(stt(r, k, -part * scale, src, ALU.mult, ALU.add))
                        src = r
                rounded(q, k, 0.25)
                do(stt(q, q, -4.0, k, ALU.mult, ALU.add))
                do(tt(z, r, r, ALU.mult))
                do(ts(p, z, 1 / 362880, -1 / 5040, ALU.mult, ALU.add))
                do(tt(p, p, z, ALU.mult))
                do(stt(p, p, 1 / 120, z, ALU.add, ALU.mult))
                do(stt(p, p, -1 / 6, z, ALU.add, ALU.mult))
                do(stt(wide["sn"], p, 1.0, r, ALU.add, ALU.mult))
                do(ts(p, z, -1 / 3628800, 1 / 40320, ALU.mult, ALU.add))
                do(tt(p, p, z, ALU.mult))
                do(stt(p, p, -1 / 720, z, ALU.add, ALU.mult))
                do(stt(p, p, 1 / 24, z, ALU.add, ALU.mult))
                do(stt(p, p, -0.5, z, ALU.add, ALU.mult))
                do(ts(wide["cs"], p, 1.0, None, ALU.add))
                do(stt(p, q, -1.0, q, ALU.mult, ALU.max))
                do(ts(k, p, -1.0, 1.0, ALU.mult, ALU.add))
                do(ts(p, p, -1.0, 2.0, ALU.mult, ALU.add))
                do(tt(q, q, p, ALU.mult))
                do(tt(cs, k, wide["cs"], ALU.mult))
                do(tt(z, q, wide["sn"], ALU.mult))
                do(tt(cs, cs, z, ALU.subtract))
                do(tt(sn, k, wide["sn"], ALU.mult))
                do(tt(z, q, wide["cs"], ALU.mult))
                do(tt(sn, sn, z, ALU.add))

            def cmul(o_re, o_im, a_re, a_im, b_re, b_im, t1, t2):
                do(tt(t1, a_re, b_re, ALU.mult))
                do(tt(t2, a_im, b_im, ALU.mult))
                do(tt(t1, t1, t2, ALU.subtract))
                do(tt(t2, a_re, b_im, ALU.mult))
                do(tt(o_im, a_im, b_re, ALU.mult))
                do(tt(o_im, o_im, t2, ALU.add))
                do(nc.vector.tensor_copy(o_re, t1))

            ldt, dt, are, aim = par["ldt"], par["dt"], par["are"], par["aim"]
            exp(dt, ldt, G)
            do(ts(are, are, -1e-4, None, ALU.min))
            do(tt(wide["arg"][:, 0:G], are, dt, ALU.mult))
            do(ts(wide["arg"][:, G:], wide["arg"][:, 0:G], float(CH), None, ALU.mult))
            do(tt(wide["ang"][:, 0:G], aim, dt, ALU.mult))
            do(ts(wide["ang"][:, G:], wide["ang"][:, 0:G], float(CH), None, ALU.mult))
            exp(wide["mag"], wide["arg"], 2 * G)
            cos_sin(wide["cw"], wide["sw2"], wide["ang"])
            do(nc.vector.tensor_copy(r8[:, :, :].rearrange("p b g -> p (b g)"), wide["mag"][:, G:]))
            pr, pi = pw_re, pw_im
            do(nc.vector.memset(pr[:, :, 8:9], 1.0))
            do(nc.vector.memset(pi[:, :, 8:9], 0.0))
            do(tt(pr[:, :, 7], wide["mag"][:, 0:G], wide["cw"][:, 0:G], ALU.mult))
            do(tt(pi[:, :, 7], wide["mag"][:, 0:G], wide["sw2"][:, 0:G], ALU.mult))
            f_re, f_im, den, num = par["f_re"], par["f_im"], par["den"], par["num"]
            t1, t2 = par["t1"], par["t2"]
            do(tt(den, are, are, ALU.mult))
            do(tt(t1, aim, aim, ALU.mult))
            do(tt(den, den, t1, ALU.add))
            do(nc.vector.reciprocal(t2, den))
            do(ts(num, pr[:, :, 7], -1.0, None, ALU.add))
            do(tt(f_re, num, are, ALU.mult))
            do(tt(t1, pi[:, :, 7], aim, ALU.mult))
            do(tt(f_re, f_re, t1, ALU.add))
            do(tt(f_re, f_re, t2, ALU.mult))
            do(tt(f_im, pi[:, :, 7], are, ALU.mult))
            do(tt(t1, num, aim, ALU.mult))
            do(tt(f_im, f_im, t1, ALU.subtract))
            do(tt(f_im, f_im, t2, ALU.mult))

            def power(dst, src, by, n):
                wideb = lambda a: a[:, :, by:by + 1].broadcast_to((P, G, n))
                cmul(pr[:, :, dst:dst + n], pi[:, :, dst:dst + n], pr[:, :, src:src + n], pi[:, :, src:src + n],
                     wideb(pr), wideb(pi), tmp_a[:, :, 0:n], tmp_b[:, :, 0:n])

            power(6, 7, 7, 1)
            power(4, 6, 6, 2)
            power(0, 4, 4, 4)
            bf = lambda a: a.unsqueeze(2).broadcast_to((P, G, 8))
            cmul(coef[:, :, 0:8], coef[:, :, 8:16], pr[:, :, 1:9], pi[:, :, 1:9], bf(f_re), bf(f_im),
                 tmp_a[:, :, :], tmp_b[:, :, :])
            do(ts(coef[:, :, 8:16], coef[:, :, 8:16], sign, -1.0, ALU.mult, ALU.mult))
            do(ts(coef[:, :, 16:24], pr[:, :, 0:8], sign, None, ALU.mult))
            do(ts(coef[:, :, 24:32], pi[:, :, 0:8], -1.0, None, ALU.mult))
            do(nc.vector.tensor_copy(e_re[:, 0, :], wide["cw"][:, G:]))
            do(nc.vector.tensor_copy(e_im[:, 0, :], wide["sw2"][:, G:]))
            for m in range(6):
                cmul(e_re[:, m + 1, :], e_im[:, m + 1, :], e_re[:, m, :], e_im[:, m, :], e_re[:, m, :], e_im[:, m, :],
                     t1, t2)
            for at_re, at_im, first, levels in ((64, 80, 0, 4), (32, 40, 4, 3)):
                do(nc.vector.memset(coef[:, :, at_re:at_re + 1], 1.0))
                do(nc.vector.memset(coef[:, :, at_im:at_im + 1], 0.0))
                for l in range(levels):
                    n = 1 << l
                    er = e_re[:, first + l, :].unsqueeze(2).broadcast_to((P, G, n))
                    ei = e_im[:, first + l, :].unsqueeze(2).broadcast_to((P, G, n))
                    cmul(coef[:, :, at_re + n:at_re + 2 * n], coef[:, :, at_im + n:at_im + 2 * n],
                         coef[:, :, at_re:at_re + n], coef[:, :, at_im:at_im + n], er, ei,
                         tmp_a[:, :, 0:n], tmp_b[:, :, 0:n])
            do(ts(coef[:, :, 48:56], coef[:, :, 40:48], sign, None, ALU.mult))
            ts(coef[:, :, 56:64], coef[:, :, 32:40], sign, None, ALU.mult).then_inc(coef_ready, 1)

        def store_out(sp, t):
            sp.wait_ge(o_ready, t + 1)
            sp.dma_start(o_view[t], gt[t % 2][:, :]).then_inc(out_stored[t % 2], 16)

        @block.sync
        def _(sp):
            sp.sem_inc(k_stored, 16)
            sp.sem_inc(u_stored, 16)
            sp.sem_inc(y_stored, 16)
            for s in range(2):
                sp.sem_inc(yp_stored[s], 16)
                sp.sem_inc(m1_stored[s], 16)

            def load_w(w, before, slot, kt=KT):
                if before is not None:
                    sp.wait_ge(raw_free[slot], before)
                sp.dma_start(raw[slot][:, 0:kt, :], wstream_d[w][:, 0:kt, :]).then_inc(raw_in[slot], 16)

            def load_coef(b, first=False):
                sp.dma_start(cf[:, :, :], coef_d[b].rearrange("p (g f) -> p g f", f=CF)).then_inc(coef_in, 16)
                sp.dma_start(bc[:, :, :, :], bc_d[b].rearrange("p (q g h) -> p q g h", q=5, h=SG)).then_inc(coef_in, 16)

            sp.dma_start(cols[:, :], cols_d).then_inc(small_in, 16)
            sp.dma_start(consts[:, :], consts_d).then_inc(small_in, 16)
            sp.dma_start(par["are"], a_re_d).then_inc(small_in, 16)
            sp.dma_start(par["aim"], a_im_d).then_inc(small_in, 16)
            sp.dma_start(par["ldt"], log_dt_d).then_inc(small_in, 16)
            for t in range(CH):
                sp.dma_start(x_tok[:, t, :], x_view[t]).then_inc(tile_in[t], 16)
            for q in range(4):
                sp.dma_start(ada[:, 4 * q:4 * q + 4, :, :],
                             w_ada_d[4 * q:4 * q + 4].rearrange("n p k m -> p n k m")).then_inc(ada_in[q], 16)
            load_w(0, None, 0)
            load_w(1, None, 1)
            sp.wait_ge(coef_ready, 1)
            sp.dma_start(coef_d.rearrange("b p f -> p b f"),
                         coef[:, :, :].rearrange("p (b g) f -> p b (g f)", g=GB)).then_inc(coef_stored, 16)
            sp.wait_ge(coef_stored, 16)
            sp.wait_ge(mm_done, 8)
            load_coef(0)
            load_w(2, 1, 0)

            def store_u(b, kjob, i):
                sp.wait_ge(job_out[kjob % 2], half(J_POOL, 8, i, kjob) + 1)
                sp.dma_start(u_d[b], u_out[:, :]).then_inc(u_stored, 16)
                sp.wait_ge(y_done, b + 1)
                sp.wait_ge(u_stored, 16 * b + 32)

            def load_u(b):
                src = u_d[b].rearrange("(g h) (t c) -> t h g c", h=SG, t=CH)
                for t in range(CH):
                    sp.dma_start(u_in[SG * t:SG * t + SG, :, :], src[t]).then_inc(u_loaded, 16)

            def kernel_taps(b):
                sp.wait_ge(k_ready, b + 1)
                sp.dma_start(k_d[b], ks[:, :, :].rearrange("p g h -> p (g h)")).then_inc(k_stored, 16)
                sp.wait_ge(k_stored, 16 * b + 32)
                src = k_d[b].rearrange("(j h) x -> h j x", h=SG)
                for t in range(CH):
                    sp.dma_start(toep[SG * t:SG * t + SG, 0:CH - t, :, :].rearrange("p r g h -> p r (g h)"),
                                 src[:, t:CH, :]).then_inc(toep_in, 16)

            def store_y(b):
                sp.wait_ge(y_taken, b + 2)
                dst = y_d[b].rearrange("(g h) (t c) -> t h g c", h=SG, t=CH)
                for r in range(CH):
                    sp.dma_start(dst[CH - 1 - r], y_act[SG * r:SG * r + SG, :, :]).then_inc(y_stored, 16)

            def store_yp(n, k, i):
                sp.wait_ge(job_out[k % 2], half(J_POOL, 8, i, k) + 1)
                sp.dma_start(yp_d[n], rt[k % 2][:, :]).then_inc(yp_stored[k % 2], 16)

            def prefetch1(i, k):
                w = k + 3
                load_w(W_POOL + 8 * i + w, half(W_POOL, 8, i, w), w % 2, 2 if w in (6, 7) else KT)

            def turn1(i, last):
                prefetch1(i, 0)
                store_u(2 * i, 0, i)
                load_u(2 * i)
                kernel_taps(2 * i)
                prefetch1(i, 1)
                sp.wait_ge(wout_ready, 2 * i + 1)
                load_coef(2 * i + 1)
                prefetch1(i, 2)
                prefetch1(i, 3)
                store_u(2 * i + 1, 3, i)
                prefetch1(i, 4)
                store_y(2 * i)
                load_u(2 * i + 1)
                kernel_taps(2 * i + 1)
                prefetch1(i, 5)
                sp.wait_ge(wout_ready, 2 * i + 2)
                if not last:
                    load_coef(2 * i + 2)
                prefetch1(i, 6)
                store_yp(2 * i, 6, i)
                prefetch1(i, 7)
                store_yp(2 * i + 1, 7, i)
                store_y(2 * i + 1)

            with sp.Fori(0, 3) as i:
                turn1(i, False)
            turn1(3, True)

            def store_gs(n, j):
                sp.wait_ge(job_out[j % 2], j // 2 + 1)
                sp.dma_start(gs_d[n], gt[j % 2][:, :]).then_inc(gs_stored[j % 2], 16)

            def load_input(src, turn):
                for n in range(KT):
                    sp.dma_start(in_raw[:, n, :], src[n]).then_inc(tile_in[n], 16)

            def next_w(w):
                load_w(w, w // 2, w % 2)

            sp.wait_ge(mm_done, J_F1)
            for s in range(2):
                sp.wait_ge(yp_stored[s], 16 * 4 + 16)
            sp.wait_ge(y_stored, 16 * CH * KT + 16)
            sp.wait_ge(sq_ready, KT)
            load_input(yp_d, 1)
            next_w(W_F1 + 3)
            store_gs(0, J_F1)
            next_w(W_F1 + 4)
            store_gs(1, J_F1 + 1)
            with sp.Fori(0, 4) as i:
                for k in range(6):
                    w = k + 3
                    load_w(W_BP + 6 * i + w, half(W_BP, 6, i, w), w % 2)
                    if k in (1, 5):
                        q = k // 4
                        sp.wait_ge(job_out[1], half(J_BP, 4, i, 2 * q + 1) + 1)
                        sp.dma_start(m1_d[2 * i + q], rt[q][:, :]).then_inc(m1_stored[q], 16)
            sp.wait_ge(mm_done, J_F2)
            load_input(y_d, 2)
            next_w(W_F2 + 3)
            store_gs(2, J_F2)
            next_w(W_F2 + 4)
            store_gs(3, J_F2 + 1)
            sp.wait_ge(row_ready, 1)
            sp.wait_ge(m1_stored[1], 16 * 5)
            for q in range(2):
                sp.dma_start(rt[q][:, :], y_d[q]).then_inc(reload_in[q], 16)

            def turn3(i, last):
                for k in range(4):
                    w = k + 3
                    load_w(W_GLU + 4 * i + w, half(W_GLU, 4, i, w), w % 2)
                    if k in (1, 3) and not last:
                        q = k // 2
                        sp.wait_ge(gated, 2 * i + q + 3)
                        sp.dma_start(rt[q][:, :], y_d[2 * i + q + 2]).then_inc(reload_in[q], 16)

            with sp.Fori(0, 3) as i:
                turn3(i, False)
            turn3(3, True)
            sp.wait_ge(mm_done, J_F3)
            sp.wait_ge(gated, KT + 2)
            for n in range(KT):
                sp.dma_start(wo_raw[:, n, :], w_out_d[n * P:n * P + P, :]).then_inc(tile_in[n], 16)
            for n in range(2):
                sp.dma_start(rt[n][:, :], m1_d[n]).then_inc(reload_in[n], 16)
            for q in range(4):
                next_w(W_F3 + q + 3)
                store_gs(4 + q, J_F3 + q)
            for s in range(2):
                sp.wait_ge(gs_stored[s], 16 * 4)
                sp.dma_start(gt[s][:, :], gs_d[s]).then_inc(g_in[s], 16)
            for n in range(KT):
                if W_BS + n + 3 < W_ALL:
                    next_w(W_BS + n + 3)
                sp.wait_ge(m_lo_done, n + 1)
                if n + 2 < KT:
                    sp.dma_start(rt[n % 2][:, :], m1_d[n + 2]).then_inc(reload_in[n % 2], 16)
                    sp.dma_start(gt[n % 2][:, :], gs_d[n + 2]).then_inc(g_in[n % 2], 16)
            for t in range(CH):
                if t >= 2:
                    store_out(sp, t - 2)
                sp.dma_start(rt[t % 2][:, :], x_view[t]).then_inc(reload_in[t % 2], 16)
            for t in range(CH - 2, CH):
                store_out(sp, t)
            for s in range(2):
                sp.wait_ge(out_stored[s], 16 * 4)

        @block.gpsimd
        def _(pool):
            steps = Steps(pool, pool_step)
            tt = nc.gpsimd.tensor_tensor

            def bcast(ap, axis, n):
                shape = list(ap.shape)
                shape.insert(axis, n)
                return ap.unsqueeze(axis).broadcast_to(tuple(shape))

            def batch(b):
                pool.wait_ge(coef_in, 32 * b + 32)
                pool.wait_ge(a_done, b + 1)
                steps.did(tt(vt[:, :, :, :], bcast(cf[:, :, 8:16], 3, SG), bcast(bc[:, 1, :, :], 2, CH), ALU.mult))
                steps.did(nc.gpsimd.tensor_scalar(cc[:, :, :], bc[:, 2, :, :], sign, None, ALU.mult))
                steps.do(tt(v[:, :, :, :], bcast(cf[:, :, 0:8], 3, SG), bcast(bc[:, 0, :, :], 2, CH), ALU.mult))
                tt(v[:, :, :, :], v[:, :, :, :], vt[:, :, :, :], ALU.add).then_inc(v_ready, 1)
                ear, eai = cf[:, :, 32:40], cf[:, :, 40:48]
                sai, sar = cf[:, :, 48:56], cf[:, :, 56:64]
                ebr, ebi = cf[:, :, 64:80], cf[:, :, 80:96]
                cos4 = cos_t[:, :, :].rearrange("p g (a b) -> p g a b", b=16)
                sin4 = sin_t[:, :, :].rearrange("p g (a b) -> p g a b", b=16)
                vt4 = vt[:, :, :, :]
                pool.wait_ge(v_ready, b + 1)
                pool.wait_ge(tables_used, b + 1)
                steps.did(tt(cos4, bcast(ear, 3, 16), bcast(ebr, 2, 8), ALU.mult))
                steps.do(tt(vt4, bcast(eai, 3, 16), bcast(ebi, 2, 8), ALU.mult))
                steps.do(tt(cos4, cos4, vt4, ALU.subtract))
                steps.did(tt(sin4, bcast(sai, 3, 16), bcast(ebr, 2, 8), ALU.mult))
                steps.do(tt(vt4, bcast(sar, 3, 16), bcast(ebi, 2, 8), ALU.mult))
                tt(sin4, sin4, vt4, ALU.add).then_inc(tables_ready, 1)
                pool.wait_ge(tables_ready, b + 1)
                pool.wait_ge(y_done, b + 1)
                steps.did(tt(vt4, bcast(cf[:, :, 24:32], 3, SG), bcast(bc[:, 3, :, :], 2, CH), ALU.mult))
                steps.do(tt(wout[:, :, :, :], bcast(cf[:, :, 16:24], 3, SG), bcast(bc[:, 2, :, :], 2, CH), ALU.mult))
                tt(wout[:, :, :, :], wout[:, :, :, :], vt4, ALU.add).then_inc(wout_ready, 1)
                pool.wait_ge(wout_ready, b + 1)

            with pool.Fori(0, KT) as b:
                steps.loop(b, 10)
                batch(b)
            steps.end(KT)

        @block.scalar
        def _(act):
            fn = nc.scalar.activation

            def split_hi(j, before, slot, kt=KT, first=False):
                act.wait_ge(raw_in[slot], 16 * before + 16)
                if not first:
                    act.wait_ge(mm_done, j - 1)
                fn(w_hi[slot][:, 0:kt, :], raw[slot][:, 0:kt, :], ACT.Copy).then_inc(hi_done, 1)

            act.wait_ge(small_in, 16 * 5)
            fn(silu_c[:, :], c_in, ACT.Silu).then_inc(silu_c_ready, 1)
            fn(glub[:, :], glu_b, ACT.Copy, scale=0.5).then_inc(silu_c_ready, 1)
            for t in range(CH):
                act.wait_ge(tile_in[t], 16)
                fn(gt[t % 2][:, :], x_tok[:, t, :], ACT.Square, accum_out=stat[:, 0, t:t + 1]).then_inc(x_sums, 1)
                if t < CH - 1:
                    act.wait_ge(x_sums, t + 1)
            act.wait_ge(x_var, 1)
            fn(stat[:, 2, :], stat[:, 1, :], ACT.Sqrt).then_inc(x_root, 1)
            split_hi(J_POOL, 0, 0, first=True)
            act.wait_ge(mod_ready, 2)
            for k in range(KT):
                act.wait_ge(mm_done, k + 1)
                if k >= 2:
                    act.wait_ge(h_done, k - 1)
                fn(gt[k % 2][:, :], ps[k % 2][:, :], ACT.Identity, bias=s_col[:, k:k + 1],
                   scale=g_col[:, k:k + 1]).then_inc(job_out[k % 2], 1)
            act.wait_ge(h_done, KT)
            act.wait_ge(pads_ready, 6)

            def evac(j, slot, dst, func, **kw):
                act.wait_ge(mm_done, j + 1)
                src = ps[slot][:, :]
                if len(dst.shape) == 3:
                    src = src.rearrange("p (t c) -> p t c", c=NC)
                fn(dst, src, func, **kw).then_inc(job_out[slot], 1)

            def a_out(b):
                act.wait_ge(a_done, b + 2)
                fn(win[:, :, :].rearrange("p g q -> p (g q)"), psa[:, :], ACT.Copy).then_inc(win_ready, 1)
                act.wait_ge(k_stored, 16 * b + 16)
                fn(ks[:, :, :].rearrange("p g h -> p (g h)"), psb[:, 0:P], ACT.Copy).then_inc(k_taken, 1)

            def swap_x(b):
                act.wait_ge(x_done, b + 1)
                sw2 = sw[:, :, :].rearrange("p g c -> p (g c)")
                fn(sw2[0:NS, :], psa[NS:P, :], ACT.Copy)
                fn(sw2[NS:P, :], psa[0:NS, :], ACT.Copy).then_inc(swapped, 1)

            def order_taps(b):
                act.wait_ge(toep_in, 16 * CH * b + 16 * CH)
                act.wait_ge(y_done, b + 1)
                fn(taps[:, :, :, :], toep[:, :, :, :].rearrange("p r g h -> p g r h"), ACT.Copy).then_inc(taps_ready, 1)

            def swap_z(b):
                act.wait_ge(z_ready, b + 1)
                fn(sw[0:NS, :, :], st[NS:P, :, :], ACT.Copy)
                fn(sw[NS:P, :, :], st[0:NS, :, :], ACT.Copy).then_inc(swapped, 1)

            def y_out(b):
                act.wait_ge(y_done, b + 2)
                act.wait_ge(y_stored, 16 * CH * b + 16)
                fn(y_act[:, :, :].rearrange("p g c -> p (g c)"), psb[:, :], ACT.Gelu_apprx_tanh).then_inc(y_taken, 1)

            def pool_high(n, q, i):
                act.wait_ge(pooled, n + 2)
                if q == 0:
                    act.wait_ge(mm_done, 8 * i + J_POOL)
                fn(pool_hi[:, q, :].rearrange("p (t c) -> p t c", c=NC), pa[:, :, 1:NC + 1], ACT.Copy).then_inc(pool_hi_done, 1)

            with act.Fori(0, 4) as i:
                def hi(k):
                    split_hi(J_POOL + 8 * i + k, half(W_POOL, 8, i, k), k % 2, 2 if k in (6, 7) else KT)

                for q in range(2):
                    n = 2 * i + q
                    k0 = 3 * q
                    hi(k0 + 1)
                    if q:
                        y_out(n - 1)
                    act.wait_ge(u_stored, 16 * n + 16)
                    evac(J_POOL + 8 * i + k0, k0 % 2, u_out[:, :], ACT.Copy)
                    a_out(n)
                    hi(k0 + 2)
                    act.wait_ge(pooled, n + 1)
                    evac(J_POOL + 8 * i + k0 + 1, (k0 + 1) % 2,
                         pu[:, :, 1:NC + 1], ACT.Copy)
                    hi(k0 + 3)
                    if q == 0:
                        swap_x(n)
                        pool_high(n, q, i)
                    else:
                        pool_high(n, q, i)
                        swap_x(n)
                    order_taps(n)
                    evac(J_POOL + 8 * i + k0 + 2, (k0 + 2) % 2, gt[q][:, :], ACT.Silu)
                    if q == 0:
                        swap_z(n)
                hi(7)
                swap_z(2 * i + 1)
                hi(8)
                y_out(2 * i + 1)

            def split_input(done):
                for n in range(KT):
                    act.wait_ge(tile_in[n], 16 * (done + 2))
                    fn(in_hi[:, n, :], in_raw[:, n, :], ACT.Copy).then_inc(in_hi_done, 1)

            def hi_at(w, j):
                split_hi(j, w // 2, w % 2)

            def gate_job(j, n):
                if n >= 2:
                    act.wait_ge(gs_stored[n % 2], 16 * (n // 2))
                evac(j, j % 2, gt[j % 2][:, :], ACT.Tanh, scale=0.5)

            hi_at(W_F1 + 1, J_F1 + 1)
            gate_job(J_F1, 0)
            hi_at(W_F1 + 2, J_F1 + 2)
            split_input(0)
            gate_job(J_F1 + 1, 1)
            for s in range(2):
                act.wait_ge(gs_stored[s], 16)
            with act.Fori(0, 4) as i:
                def hi2(k, w=None):
                    w = k if w is None else w
                    split_hi(J_BP + 4 * i + k, half(W_BP, 6, i, w), k % 2)

                hi2(1)
                evac(J_BP + 4 * i, 0, gt[0][:, :], ACT.Tanh, scale=0.5)
                hi2(2)
                hi2(3, 5)
                evac(J_BP + 4 * i + 2, 0, gt[1][:, :], ACT.Tanh, scale=0.5)
                hi2(4, 6)
            hi_at(W_F2 + 1, J_F2 + 1)
            gate_job(J_F2, 2)
            hi_at(W_F2 + 2, J_F2 + 2)
            act.wait_ge(mm_done, J_F2)
            split_input(1)
            gate_job(J_F2 + 1, 3)
            act.wait_ge(row_done, 1)
            fn(gate_row[:, :], psa[:, :], ACT.Copy).then_inc(row_ready, 1)
            for s in range(2):
                act.wait_ge(gs_stored[s], 32)
            with act.Fori(0, 4) as i:
                def hi3(k):
                    split_hi(J_GLU + 4 * i + k, half(W_GLU, 4, i, k), k % 2)

                for q in range(2):
                    n = 2 * i + q
                    hi3(2 * q + 1)
                    act.wait_ge(gated, n + 1)
                    evac(J_GLU + 4 * i + 2 * q, 0, gt[q][:, :], ACT.Silu)
                    hi3(2 * q + 2)
                    evac(J_GLU + 4 * i + 2 * q + 1, 1, ys_raw[:, n, :], ACT.Tanh, scale=0.5,
                         bias=glub[:, bass.ds(n, 1)])
            hi_at(W_F3 + 1, J_F3 + 1)
            act.wait_ge(mm_done, J_F3)
            act.wait_ge(gated, KT + 2)
            for n in range(KT):
                fn(in_hi[:, n, :], ys_raw[:, n, :], ACT.Copy).then_inc(in_hi_done, 1)
            for q in range(4):
                gate_job(J_F3 + q, 4 + q)
                if q < 3:
                    hi_at(W_F3 + q + 2, J_F3 + q + 2)

            def m_high(n, q):
                act.wait_ge(m_sum, n + 1)
                fn(m_hi[:, n, :], rt[q][:, :], ACT.Copy).then_inc(m_hi_done, 1)

            def turn4(i, last):
                for q in range(2):
                    if not (last and q == 1):
                        split_hi(J_BS + 2 * i + q + 1, half(W_BS, 2, i, q + 1), (q + 1) % 2)
                    m_high(2 * i + q, q)

            with act.Fori(0, 3) as i:
                turn4(i, False)
            turn4(3, True)
            for n in range(KT):
                act.wait_ge(tile_in[n], 16 * 4)
                fn(wo_hi[:, n, :], wo_raw[:, n, :], ACT.Copy).then_inc(in_hi_done, 1)
            for t in range(CH):
                act.wait_ge(mm_done, J_OUT + t + 1)
                if t:
                    act.wait_ge(o_sums, t)
                fn(squares[:, :], ps[t % 2][:, :], ACT.Square, accum_out=stat[:, 0, t:t + 1]).then_inc(o_sums, 1)
                act.wait_ge(o_var, t + 1)
                fn(stat[:, 2, t:t + 1], stat[:, 1, t:t + 1], ACT.Sqrt).then_inc(o_root, 1)

        @block.vector
        def _(dve):
            tt, stt = nc.vector.tensor_tensor, nc.vector.scalar_tensor_tensor
            ts = nc.vector.tensor_scalar
            steps = Steps(dve, dve_step)
            do, did = steps.do, steps.did

            def split_lo(j, slot, kt=KT):
                dve.wait_ge(hi_done, j - 7)
                tt(w_lo[slot][:, 0:kt, :], raw[slot][:, 0:kt, :], w_hi[slot][:, 0:kt, :].bitcast(F32),
                   ALU.subtract).then_inc(raw_free[slot], 1)

            dve.wait_ge(small_in, 16 * 5)
            coefficients(dve, steps)
            dve.wait_ge(x_sums, CH)
            ts(stat[:, 1, :], stat[:, 0, :], 1.0 / D, EPS, ALU.mult, ALU.add).then_inc(x_var, 1)
            dve.wait_ge(x_root, 1)
            newton(steps, slice(0, CH), 1.0)
            for t in range(CH):
                ts(x_tok[:, t, :], x_tok[:, t, :], stat[:, 4, t:t + 1], None, ALU.mult).then_inc(x_scaled, 1)
            split_lo(J_POOL, 0)
            dve.wait_ge(mod_done, 1)
            tt(s_col[:, :], psb[:, 0:KT], b_ada[:, 0:KT], ALU.add).then_inc(mod_ready, 1)
            do(tt(g_col[:, :], psb[:, KT:2 * KT], b_ada[:, KT:2 * KT], ALU.add))
            stt(g_col[:, :], g_col[:, :], 1.0, npre, ALU.add, ALU.mult).then_inc(mod_ready, 1)
            dve.sem_inc(y_taken, 1)
            for k in range(KT):
                dve.wait_ge(job_out[k % 2], k // 2 + 1)
                did(nc.vector.tensor_copy(h_hi[:, k, :], gt[k % 2][:, :]))
                steps.landed()
                tt(h_lo[:, k, :], gt[k % 2][:, :], h_hi[:, k, :].bitcast(F32), ALU.subtract).then_inc(h_done, 1)
            dve.wait_ge(coef_stored, 16)
            nc.vector.memset(toep[:, :, :, :], 0.0).then_inc(pads_ready, 1)
            nc.vector.memset(sq[:, :, 0:1], 0.0).then_inc(pads_ready, 1)
            for z in (pu, pa, pb):
                nc.vector.memset(z[:, :, 0:1], 0.0).then_inc(pads_ready, 1)
            nc.vector.memset(ones[:, :], 1.0).then_inc(pads_ready, 1)
            dve.wait_ge(pads_ready, 6)
            dve.sem_inc(pooled, 1)
            dve.sem_inc(tables_used, 1)
            dve.sem_inc(x_taken, 1)

            def lo(i, k):
                split_lo(8 * i + J_POOL + k, k % 2, 2 if k in (6, 7) else KT)

            def d_skip(b):
                dve.wait_ge(k_taken, b + 1)
                do(tt(dk[96:P, :, :], bc[96:P, 4, :, :], dmask[96:P, :].unsqueeze(1).broadcast_to((32, GB, SG)),
                      ALU.mult))
                tt(ks[96:P, :, :], ks[96:P, :, :], dk[96:P, :, :], ALU.add).then_inc(k_ready, 1)

            def rotate_in(b):
                flat = lambda a: a[:, :, :].rearrange("p g c -> p (g c)")
                dve.wait_ge(tables_ready, b + 1)
                dve.wait_ge(swapped, 2 * b + 1)
                did(tt(flat(sw), flat(sw), flat(sin_t), ALU.mult))
                tt(flat(st), psa[:, :], flat(cos_t), ALU.mult).then_inc(x_taken, 1)
                dve.wait_ge(x_taken, b + 2)
                steps.landed()
                do(tt(flat(st), flat(st), flat(sw), ALU.add))
                for g in range(GB):
                    ins = nc.vector.tensor_tensor_scan(st[:, g, :], r8[:, b, g:g + 1].broadcast_to((P, NC)),
                                                       st[:, g, :], 0.0, ALU.mult, ALU.add)
                    if g < GB - 1:
                        did(ins)
                ins.then_inc(z_ready, 1)

            def rotate_out(b):
                flat = lambda a: a[:, :, :].rearrange("p g c -> p (g c)")
                dve.wait_ge(swapped, 2 * b + 2)
                did(tt(flat(sw), flat(sw), flat(sin_t), ALU.mult))
                tt(flat(st), flat(st), flat(cos_t), ALU.mult).then_inc(tables_used, 1)
                dve.wait_ge(tables_used, b + 2)
                steps.landed()
                tt(sq[:, :, 1:NC], st[:, :, 0:NC - 1], sw[:, :, 0:NC - 1], ALU.subtract).then_inc(sq_ready, 1)

            def pooling(n, q, i, slot, jk):
                dve.wait_ge(job_out[slot], half(J_POOL, 8, i, jk) + 1)
                bufs = [pu, pa, pb, pa, pb]
                for l in range(LEVELS):
                    s, o, d = bufs[l], bufs[l + 1], 1 << l
                    on = level_on[:, i, l:l + 1]
                    if d < CH:
                        did(stt(o[:, d:CH, 1:NC + 1], s[:, 0:CH - d, 1:NC + 1], on, s[:, d:CH, 1:NC + 1],
                                ALU.mult, ALU.add))
                    do(stt(o[:, 0:d, 1:NC + 1], s[:, CH - d:CH, 0:NC], on, s[:, 0:d, 1:NC + 1],
                           ALU.mult, ALU.add))
                did(stt(pa[:, :, 1:NC + 1], pb[:, :, 1:NC + 1], inv_w[:, bass.ds(i, 1)], pu[:, :, 1:NC + 1],
                        ALU.mult, ALU.subtract))
                do(tt(pfix[:, :, :], pb[:, :, 1:3], inv_n[:, i, :, :], ALU.mult))
                tt(pa[:, :, 1:3], pfix[:, :, :], pu[:, :, 1:3], ALU.subtract).then_inc(pooled, 1)
                dve.wait_ge(pool_hi_done, n + 1)
                tt(pool_lo[:, q, :].rearrange("p (t c) -> p t c", c=NC), pa[:, :, 1:NC + 1],
                   pool_hi[:, q, :].bitcast(F32).rearrange("p (t c) -> p t c", c=NC),
                   ALU.subtract).then_inc(pool_lo_done, 1)

            def yp_out(i, q):
                k = 6 + q
                dve.wait_ge(mm_done, 8 * i + J_POOL + k + 1)
                dve.wait_ge(yp_stored[q], 16 * i + 16)
                stt(rt[q][:, :], ps[q][:, :], pscale[:, bass.ds(2 * i + q, 1)], gt[q][:, :],
                    ALU.mult, ALU.mult).then_inc(job_out[q], 1)

            with dve.Fori(0, 4) as i:
                steps.loop(i, 40)
                n = 2 * i
                lo(i, 1)
                d_skip(n)
                lo(i, 2)
                lo(i, 3)
                rotate_in(n)
                pooling(n, 0, i, 1, 1)
                lo(i, 4)
                rotate_out(n)
                n = 2 * i + 1
                d_skip(n)
                lo(i, 5)
                lo(i, 6)
                pooling(n, 1, i, 0, 4)
                rotate_in(n)
                lo(i, 7)
                rotate_out(2 * i + 1)
                lo(i, 8)
                yp_out(i, 0)
                yp_out(i, 1)
            steps.end(4)

            def lo_at(w, j):
                split_lo(j, w % 2)

            def split_input(base):
                for n in range(KT):
                    dve.wait_ge(in_hi_done, base + n + 1)
                    tt(in_lo[:, n, :], in_raw[:, n, :], in_hi[:, n, :].bitcast(F32),
                       ALU.subtract).then_inc(in_lo_done, 1)

            lo_at(W_F1 + 1, J_F1 + 1)
            lo_at(W_F1 + 2, J_F1 + 2)
            split_input(0)
            dve.sem_inc(gate_taken, 2)
            with dve.Fori(0, 4) as i:
                def lo2(k):
                    split_lo(4 * i + J_BP + k, k % 2)

                def m1_out(q):
                    k = 2 * q + 1
                    dve.wait_ge(job_out[0], half(J_BP, 4, i, 2 * q) + 1)
                    dve.wait_ge(mm_done, 4 * i + J_BP + k + 1)
                    dve.wait_ge(m1_stored[q], 16 * i + 16)
                    stt(rt[q][:, :], gt[q][:, :], 1.0, ps[1][:, :], ALU.add, ALU.mult).then_inc(job_out[1], 1)

                lo2(1)
                lo2(2)
                m1_out(0)
                for q in range(2):
                    dve.wait_ge(raw_free[1 - q], half(W_BP, 6, i, 3 + q) + 1)
                for q in range(2):
                    stt(gate_col[:, bass.ds(2 * i + q, 1)], psb[:, q:q + 1], b_ada[:, bass.ds(2 * i + q + 16, 1)],
                        npost[:, bass.ds(2 * i + q, 1)], ALU.add, ALU.mult).then_inc(gate_taken, 1)
                lo2(3)
                lo2(4)
                m1_out(1)
            lo_at(W_F2 + 1, J_F2 + 1)
            dve.wait_ge(gate_taken, KT + 2)
            dve.wait_ge(m1_stored[0], 16 * 5)
            for k in range(KT):
                ts(rt[0][:, k * P:k * P + P], ident, gate_col[:, k:k + 1], None, ALU.mult).then_inc(diag_ready, 1)
            lo_at(W_F2 + 2, J_F2 + 2)
            split_input(KT)
            dve.sem_inc(gated, 2)
            with dve.Fori(0, 4) as i:
                steps.loop(i, 2)

                def lo3(k):
                    split_lo(4 * i + J_GLU + k, k % 2)

                for q in range(2):
                    n = 2 * i + q
                    lo3(2 * q + 1)
                    lo3(2 * q + 2)
                    dve.wait_ge(reload_in[q], 16 * i + 16)
                    dve.wait_ge(job_out[0], half(J_GLU, 4, i, 2 * q) + 1)
                    dve.wait_ge(job_out[1], half(J_GLU, 4, i, 2 * q + 1) + 1)
                    do(stt(ys_raw[:, n, :], ys_raw[:, n, :], 1.0, rt[q][:, :], ALU.add, ALU.mult))
                    stt(ys_raw[:, n, :], ys_raw[:, n, :], 0.5, gt[q][:, :], ALU.mult, ALU.mult).then_inc(gated, 1)
            steps.end(4)
            lo_at(W_F3 + 1, J_F3 + 1)
            for n in range(KT):
                dve.wait_ge(in_hi_done, 2 * KT + n + 1)
                tt(ys_lo[:, n, :], ys_raw[:, n, :], in_hi[:, n, :].bitcast(F32), ALU.subtract).then_inc(in_lo_done, 1)
            for q in range(3):
                lo_at(W_F3 + q + 2, J_F3 + q + 2)

            def merge(i, q):
                n = 2 * i + q
                dve.wait_ge(g_in[q], 16 * i + 16)
                dve.wait_ge(mm_done, J_BS + n + 1)
                stt(gt[q][:, :], gt[q][:, :], 1.0, ps[q][:, :], ALU.add, ALU.mult).then_inc(job_out[q], 1)
                dve.wait_ge(job_out[q], half(J_BS, 2, i, q) + 1)
                dve.wait_ge(reload_in[q], 16 * i + 16 * 5)
                tt(rt[q][:, :], gt[q][:, :], rt[q][:, :], ALU.add).then_inc(m_sum, 1)
                dve.wait_ge(m_hi_done, n + 1)
                tt(m_lo[:, n, :], rt[q][:, :], m_hi[:, n, :].bitcast(F32), ALU.subtract).then_inc(m_lo_done, 1)

            def turn4(i, last):
                for q in range(2):
                    if not (last and q == 1):
                        split_lo(2 * i + J_BS + q + 1, (q + 1) % 2)
                    merge(i, q)

            with dve.Fori(0, 3) as i:
                turn4(i, False)
            turn4(3, True)
            for n in range(KT):
                dve.wait_ge(in_hi_done, 3 * KT + n + 1)
                tt(wo_lo[:, n, :], wo_raw[:, n, :], wo_hi[:, n, :].bitcast(F32), ALU.subtract).then_inc(in_lo_done, 1)
            for t in range(CH):
                one = slice(t, t + 1)
                dve.wait_ge(o_sums, t + 1)
                ts(stat[:, 1, one], stat[:, 0, one], 0.25 / D, EPS, ALU.mult, ALU.add).then_inc(o_var, 1)
                dve.wait_ge(o_root, t + 1)
                newton(steps, one, 0.5)
                if t == 0:
                    dve.wait_ge(row_ready, 1)
                if t >= 2:
                    dve.wait_ge(out_stored[t % 2], 16 * (t // 2))
                stt(gt[t % 2][:, :], ps[t % 2][:, :], stat[:, 4, one], gate_row[:, :],
                    ALU.mult, ALU.mult).then_inc(job_out[t % 2], 1)
                dve.wait_ge(job_out[t % 2], (J_OUT + t) // 2 + 1)
                dve.wait_ge(reload_in[t % 2], 16 * (9 + t // 2))
                tt(gt[t % 2][:, :], gt[t % 2][:, :], rt[t % 2][:, :], ALU.add).then_inc(o_ready, 1)

        @block.tensor
        def _(pe):
            mm = nc.tensor.matmul
            pe.sem_inc(a_done, 1)
            pe.sem_inc(y_done, 1)

            pe.wait_ge(silu_c_ready, 1)
            for n in range(2 * KT):
                if n % 4 == 0:
                    pe.wait_ge(ada_in[n // 4], 16)
                for k in range(KT):
                    last = mm(psb[:, n:n + 1], ada[:, n, k, :], silu_c[:, k:k + 1], start=k == 0, stop=k == KT - 1)
            last.then_inc(mod_done, 1)
            pe.wait_ge(x_scaled, CH)
            for k in range(KT):
                if k >= 2:
                    pe.wait_ge(job_out[k % 2], k // 2)
                for t in range(CH):
                    last = nc.tensor.transpose(ps[k % 2][:, t * P:t * P + P], x_tok[:, t, k * P:k * P + P], ident)
                last.then_inc(mm_done, 1)

            def product(j, before, slot, x_hi, x_lo, kt=KT):
                pe.wait_ge(hi_done, j - 7)
                pe.wait_ge(job_out[slot], before)
                for k in range(kt):
                    for q, (a, b) in enumerate(((w_hi, x_hi), (w_hi, x_lo), (w_lo, x_hi))):
                        for f in range(2):
                            last = mm(ps[slot][:, f * HALF:f * HALF + HALF], a[slot][:, k, :],
                                      b[:, k, f * HALF:f * HALF + HALF],
                                      start=k == 0 and q == 0, stop=k == kt - 1 and q == 2)
                last.then_inc(mm_done, 1)

            pe.wait_ge(h_done, KT)

            def part_a(b):
                pe.wait_ge(v_ready, b + 1)
                pe.wait_ge(x_taken, b + 1)
                pe.wait_ge(y_taken, b + 1)
                for g in range(GB):
                    vg = v[:, g, :, :].rearrange("p j h -> p (j h)")
                    mm(psb[:, g * SG:g * SG + SG], vg, cc[:, g, :], start=True, stop=True)
                for g in range(GB):
                    vg = v[:, g, :, :].rearrange("p j h -> p (j h)")
                    last = nc.tensor.transpose(psa[:, g * P:g * P + P], vg, ident)
                last.then_inc(a_done, 1)

            def part_b(b):
                pe.wait_ge(win_ready, b + 1)
                pe.wait_ge(u_loaded, 16 * CH * b + 16 * CH)
                for g in range(GB):
                    last = mm(psa[:, g * P:g * P + P], win[:, g, :], u_in[:, g, :], start=True, stop=True)
                last.then_inc(x_done, 1)

            def part_c(b):
                pe.wait_ge(sq_ready, b + 1)
                pe.wait_ge(wout_ready, b + 1)
                pe.wait_ge(k_taken, b + 1)
                pe.wait_ge(taps_ready, b + 1)
                for g in range(GB):
                    mm(psb[:, g * P:g * P + P], taps[:, g, :, :].rearrange("p r h -> p (r h)"), u_in[:, g, :], start=True, stop=False)
                    last = mm(psb[:, g * P:g * P + P], wout[:, g, :, :].rearrange("p r h -> p (r h)"), sq[:, g, :],
                              start=False, stop=True)
                last.then_inc(y_done, 1)

            with pe.Fori(0, 4) as i:
                def job(k):
                    if k in (6, 7):
                        if k == 6:
                            pe.wait_ge(pool_lo_done, 2 * i + 2)
                        xs, kt = (pool_hi, pool_lo), 2
                    else:
                        xs, kt = (h_hi, h_lo), KT
                    pe.wait_ge(raw_free[k % 2], half(W_POOL, 8, i, k) + 1)
                    product(8 * i + J_POOL + k, half(J_POOL, 8, i, k), k % 2, *xs, kt)

                for q in range(2):
                    job(3 * q)
                    if q:
                        part_c(2 * i)
                    part_a(2 * i + q)
                    job(3 * q + 1)
                    part_b(2 * i + q)
                    job(3 * q + 2)
                job(6)
                job(7)
                part_c(2 * i + 1)

            def plain(j, w, xs):
                pe.wait_ge(raw_free[w % 2], w // 2 + 1)
                product(j, j // 2, j % 2, *xs)

            h = (h_hi, h_lo)
            for q in range(2):
                plain(J_F1 + q, W_F1 + q, h)
            pe.wait_ge(in_lo_done, KT)
            pe.wait_ge(y_taken, KT + 1)
            with pe.Fori(0, 4) as i:
                def job2(k, w, xs):
                    pe.wait_ge(raw_free[k % 2], half(W_BP, 6, i, w) + 1)
                    product(4 * i + J_BP + k, half(J_BP, 4, i, k), k % 2, *xs)

                job2(0, 0, h)
                job2(1, 1, (in_hi, in_lo))
                for q in range(2):
                    pe.wait_ge(raw_in[1 - q], 16 * half(W_BP, 6, i, 3 + q) + 16)
                    if q == 0:
                        pe.wait_ge(gate_taken, 2 * i + 2)
                    for k in range(KT):
                        last = mm(psb[:, q:q + 1], raw[1 - q][:, k, :], silu_c[:, k:k + 1],
                                  start=k == 0, stop=k == KT - 1)
                    last.then_inc(raw_free[1 - q], 1)
                job2(2, 2, h)
                job2(3, 5, (in_hi, in_lo))
            for q in range(2):
                plain(J_F2 + q, W_F2 + q, h)
            pe.wait_ge(diag_ready, KT)
            for f in range(2):
                last = mm(psa[:, f * HALF:f * HALF + HALF], ones[:, :], rt[0][:, f * HALF:f * HALF + HALF],
                          start=True, stop=True)
            last.then_inc(row_done, 1)
            pe.wait_ge(in_lo_done, 2 * KT)
            with pe.Fori(0, 4) as i:
                for k in range(4):
                    pe.wait_ge(raw_free[k % 2], half(W_GLU, 4, i, k) + 1)
                    product(4 * i + J_GLU + k, half(J_GLU, 4, i, k), k % 2, *(h if k % 2 == 0 else (in_hi, in_lo)))
            for q in range(4):
                plain(J_F3 + q, W_F3 + q, h)
            pe.wait_ge(in_lo_done, 3 * KT)
            with pe.Fori(0, 4) as i:
                for k in range(2):
                    pe.wait_ge(raw_free[k % 2], half(W_BS, 2, i, k) + 1)
                    product(2 * i + J_BS + k, half(J_BS, 2, i, k), k % 2, in_hi, ys_lo)
            for t in range(CH):
                slot = t % 2
                pe.wait_ge(job_out[slot], (J_OUT + t) // 2)
                for k in range(KT):
                    if t == 0:
                        pe.wait_ge(m_lo_done, k + 1)
                        pe.wait_ge(in_lo_done, 3 * KT + k + 1)
                    for q, (a, b) in enumerate(((m_hi, wo_hi), (m_hi, wo_lo), (m_lo, wo_hi))):
                        for f in range(2):
                            last = mm(ps[slot][:, f * HALF:f * HALF + HALF], a[:, k, t * P:t * P + P],
                                      b[:, k, f * HALF:f * HALF + HALF],
                                      start=k == 0 and q == 0, stop=k == KT - 1 and q == 2)
                last.then_inc(mm_done, 1)


def kernel(x, c, w_ada, b_ada, norm_pre, norm_post, w_in, pool_w, pool_scale,
           ssm_a_re, ssm_a_im, ssm_log_dt, ssm_b_re, ssm_b_im, ssm_c_re, ssm_c_im,
           ssm_d, glu_w, glu_b, w_branch_pool, w_branch_ssm, w_out):
    import numpy as np
    import concourse.bacc as bacc
    from concourse.bass_utils import run_bass_kernel_spmd

    def column(vec):
        return np.asarray(vec).reshape(-1, P).T

    def tiles(w):
        w = np.asarray(w)
        return w.reshape(w.shape[0] // P, P, w.shape[1] // P, P).transpose(2, 1, 0, 3)

    ada = tiles(w_ada[0])
    win = tiles(w_in[0])
    u_pool, z_pool, u_ssm, z_ssm, g_pool, g_ssm = (win[KT * q:KT * q + KT] for q in range(6))
    pw = np.asarray(pool_w[0])
    pool = np.zeros((KT, P, KT, P), pw.dtype)
    pool[:, :, 0:2, :] = pw.reshape(4, 2, P, 2, P).transpose(0, 3, 2, 1, 4).reshape(KT, P, 2, P)
    wbp, wbs, glu = tiles(w_branch_pool[0]), tiles(w_branch_ssm[0]), tiles(glu_w[0])
    gate = ada[2 * KT:]
    stream = []
    for i in range(4):
        a, b = 2 * i, 2 * i + 1
        stream += [u_ssm[a], u_pool[a], z_pool[a], u_ssm[b], u_pool[b], z_pool[b], pool[a], pool[b]]
    stream += [g_ssm[0], g_ssm[1]]
    for i in range(4):
        a, b = 2 * i, 2 * i + 1
        stream += [g_pool[a], wbp[a], g_pool[b], gate[a], gate[b], wbp[b]]
    stream += [g_ssm[2], g_ssm[3]]
    for i in range(4):
        a, b = 2 * i, 2 * i + 1
        stream += [z_ssm[a], glu[a], z_ssm[b], glu[b]]
    stream += [g_ssm[n] for n in range(4, 8)] + [wbs[n] for n in range(KT)]

    cols = np.concatenate([column(v) for v in (c[0], norm_pre[0], b_ada[0], norm_post[0], pool_scale[0],
                                               glu_b[0])], 1)
    consts = np.zeros((P, 232), np.float32)
    consts[:, 0:128] = np.eye(P)
    consts[:, 128] = np.where(np.arange(P) < NS, 1.0, -1.0)
    for q, w in enumerate(WINDOWS):
        consts[:, 129 + 4 * q:133 + 4 * q] = [1.0 if (2 << l) <= w else 0.0 for l in range(LEVELS)]
        consts[:, 145 + q] = 1.0 / w
        for t in range(CH):
            for ch in range(2):
                consts[:, 149 + 16 * q + 2 * t + ch] = 1.0 / min(w, 8 * ch + t + 1)
    for h in range(SG):
        consts[P - SG + h, 213 + h] = 1.0

    def stack(top, low):
        return np.concatenate([np.moveaxis(np.asarray(top), 1, 0), np.moveaxis(np.asarray(low), 1, 0)], 0)

    b_re, b_im = np.asarray(ssm_b_re[0]), np.asarray(ssm_b_im[0])
    c_re, c_im = (np.swapaxes(np.asarray(m[0]), 1, 2) for m in (ssm_c_re, ssm_c_im))
    d_all = np.broadcast_to(np.asarray(ssm_d[0]), (P, G, SG))
    bcs = np.stack([stack(b_re, b_im), stack(b_im, b_re), stack(c_re, c_im), stack(c_im, c_re), d_all], 1)
    bcs = bcs.reshape(P, 5, KT, GB * SG).transpose(2, 0, 1, 3).reshape(KT, P, 5 * GB * SG)
    arrays = {
        "x": x, "cols": cols, "consts": consts,
        "a_re": stack(ssm_a_re[0], ssm_a_re[0]), "a_im": stack(ssm_a_im[0], ssm_a_im[0]),
        "log_dt": np.broadcast_to(np.asarray(ssm_log_dt[0]), (P, G)),
        "bc": bcs, "w_ada": ada[0:2 * KT], "wstream": np.stack(stream), "w_out": w_out[0],
    }
    arrays = {f"in_{k}": np.ascontiguousarray(a) for k, a in arrays.items()}
    nc = bacc.Bacc("TRN2", target_bir_lowering=False, num_devices=1)
    args = [nc.dram_tensor(k, a.shape, mybir.dt.from_np(a.dtype), kind="ExternalInput").ap()
            for k, a in arrays.items()]
    args.append(nc.dram_tensor("out", (1, SEQ, D), F32, kind="ExternalOutput").ap())
    build(nc, *args)
    r = run_bass_kernel_spmd(nc, [arrays], core_ids=[0])
    return r.results[0]["out"]
```

```python
from contextlib import ExitStack
import concourse.bass as bass
from concourse import mybir
from concourse.alu_op_type import AluOpType as ALU

ACT = mybir.ActivationFunctionType
F32 = mybir.dt.float32
F32R = mybir.dt.float32r
I32 = mybir.dt.int32

P = 128
D = 1024
KT = D // P
SEQ = 1024
CH = 8
NC = SEQ // CH
HALF = 512
G = 64
SG = 16
NS = 64
GB = P // SG
WINDOWS = (2, 4, 8, 16)
LEVELS = 4
EPS = 1e-6
CF = 96
TILE = 4096

J_G = 0
J_P, W_P = J_G + 5, 5
J_F1, W_F1 = J_P + 4 * 8, W_P + 4 * 6
J_BP, W_BP = J_F1 + 1, W_F1 + 1
J_GLU, W_GLU = J_BP + 4 * 4, W_BP + 4 * 6
J_F3, W_F3 = J_GLU + 4 * 4, W_GLU + 4 * 4
J_BS, W_BS = J_F3 + 2, W_F3 + 2
J_OUT, W_ALL = J_BS + 4 * 2, W_BS + 4 * 2
ACT_HIGH = (0, 2, 4, 6)


def half_pi_parts():
    unit = 10 ** 35
    rest, parts = 157079632679489661923132169163975144, []
    rest <<= 34
    for bits in (10, 22, 34):
        n = rest // (unit << (34 - bits))
        parts.append(n / 2 ** bits)
        rest -= n * (unit << (34 - bits))
    return parts + [rest / (unit << 34)]


class Steps:

    def __init__(self, eng, sem):
        self.eng, self.sem, self.base, self.k, self.turn, self.per = eng, sem, 0, 0, None, 0

    def did(self, ins):
        ins.then_inc(self.sem, 1)
        self.k += 1

    def landed(self):
        v = self.base + self.k
        self.eng.wait_ge(self.sem, v if self.turn is None else self.turn * self.per + v)

    def do(self, ins):
        self.did(ins)
        self.landed()

    def loop(self, turn, per):
        self.base, self.k, self.turn, self.per = self.base + self.k, 0, turn, per

    def end(self, turns):
        assert self.k == self.per, (self.k, self.per)
        self.base, self.k, self.turn = self.base + self.per * turns, 0, None


def build(nc, x, c_d, cols_d, consts_d, a_re_d, a_im_d, log_dt_d, bc_d, w_ada_d, wstream_d, pool_d, w_out_d, out):
    ctx = ExitStack()
    with ctx:
        def sem(name):
            return ctx.enter_context(nc.semaphore(name))

        def psum(name):
            return ctx.enter_context(nc.psum_tensor(name, [P, 2 * HALF], F32))

        cur = [-(-nc.sbuf_base // 64) * 64]

        def at(name, shape, offset, dt=F32):
            return nc.alloc_sbuf_tensor_at(name, shape, dt, offset=offset)

        def nbytes(shape):
            n = 4
            for s in shape[1:]:
                n *= s
            return -(-n // 32) * 32

        def new(name, shape, dt=F32):
            t = at(name, shape, cur[0], dt)
            cur[0] += nbytes(shape)
            return t

        big = [P, KT, SEQ]
        h_hi_at = cur[0]
        h_hi = new("h_hi", big, F32R)
        h_lo = new("h_lo", big, F32R)
        ada = at("ada", [P, 2, KT, D], h_hi_at)
        m_hi = at("m_hi", big, h_hi_at, F32R)
        m_lo = at("m_lo", big, h_hi_at + 8 * TILE, F32R)
        raw_at = cur[0]
        raw = [new(f"raw{s}", [P, KT, P]) for s in range(2)]
        diag = at("diag", [P, CH, P], cur[0] + 3 * TILE)
        w_hi = [new(f"w_hi{s}", [P, KT, P], F32R) for s in range(2)]
        w_lo = [new(f"w_lo{s}", [P, KT, P], F32R) for s in range(2)]
        squares = at("squares", [P, SEQ], raw_at)
        gt = [new(f"gt{s}", [P, SEQ]) for s in range(2)]
        rt = [new(f"rt{s}", [P, SEQ]) for s in range(2)]
        a_at = cur[0]
        b_at, c_at = a_at + 8 * TILE, a_at + 16 * TILE
        cur[0] = a_at + 24 * TILE

        x_tok = at("x_tok", big, a_at)
        coef = at("coef", [P, G, CF], c_at)
        mod_out = at("mod_out", [P, 2, D], c_at + 6 * TILE)
        in_hi = at("in_hi", big, a_at, F32R)
        in_raw = at("in_raw", big, c_at)
        y_raw = at("y_raw", big, b_at)
        in_lo = at("in_lo", big, c_at, F32R)
        ys_raw = at("ys_raw", big, b_at)
        ys_lo = at("ys_lo", big, b_at, F32R)
        wo_raw = at("wo_raw", [P, KT, D], c_at)
        wo_lo = at("wo_lo", [P, KT, D], c_at, F32R)
        wo_hi_big = at("wo_hi", [P, KT, D], a_at, F32R)
        wo_hi_first = [at(f"wo_hi{n}", [P, D], raw_at + o * TILE, F32R) for n, o in enumerate((2, 4, 1))]
        wo_hi = [t[:, :] for t in wo_hi_first] + [wo_hi_big[:, n, :] for n in range(3, KT)]

        p1 = [a_at]

        def ssm(name, shape, dt=F32):
            t = at(name, shape, p1[0], dt)
            p1[0] += nbytes(shape)
            return t

        cf = ssm("cf", [P, GB, CF])
        bc = ssm("bc", [P, 5, GB, SG])
        v = ssm("v", [P, GB, CH, SG])
        vt = ssm("vt", [P, GB, CH, SG])
        wout = ssm("wout", [P, GB, CH, SG])
        cc = ssm("cc", [P, GB, SG])
        cos_t = ssm("cos_t", [P, GB, NC])
        sin_t = ssm("sin_t", [P, GB, NC])
        win = ssm("win", [P, GB, P])
        ks = ssm("ks", [P, GB, SG])
        dk = ssm("dk", [P, GB, SG])
        toep = ssm("toep", [P, CH, GB, SG])
        taps = ssm("taps", [P, GB, CH, SG])
        u_in = ssm("u_in", [P, GB, NC])
        u_out = ssm("u_out", [P, SEQ])
        st = ssm("st", [P, GB, NC])
        sw = ssm("sw", [P, GB, NC])
        sq = ssm("sq", [P, GB, NC])
        y_act = ssm("y_act", [P, GB, NC])
        pad = [P, CH, NC + 1]
        pu, pa, pb = ssm("pu", pad), ssm("pa", pad), ssm("pb", pad)
        pfix = ssm("pfix", [P, CH, 2])
        pool_hi = ssm("pool_hi", [P, 2, SEQ], F32R)
        pool_lo = ssm("pool_lo", [P, 2, SEQ], F32R)
        assert p1[0] <= cur[0], (p1[0], cur[0])

        cols = new("cols", [P, 56])
        consts = new("consts", [P, 232])
        mod_acc = new("mod_acc", [P, 2 * KT])
        g_col = new("g_col", [P, KT])
        s_col = new("s_col", [P, KT])
        gate_col = new("gate_col", [P, KT])
        glub = new("glub", [P, KT])
        r8 = new("r8", [P, KT, GB])
        stat = new("stat", [P, 6, 8])
        ones = at("ones", [P, P], cur[0])
        pw_raw = new("pw_raw", [P, 4, P])
        gate_row = at("gate_row", [P, D], cur[0])
        silu_row = at("silu_row", [P, D], cur[0])
        pw_hi = new("pw_hi", [P, 4, P], F32R)
        pw_lo = new("pw_lo", [P, 4, P], F32R)
        assert cur[0] <= nc.sbuf_usable_end, cur[0]

        npre, b_ada = cols[:, 0:8], cols[:, 8:32]
        npost, pscale, glu_b = cols[:, 32:40], cols[:, 40:48], cols[:, 48:56]
        ident = consts[:, 0:128]
        sign = consts[:, 128:129]
        level_on = consts[:, 129:145].rearrange("p (g l) -> p g l", l=LEVELS)
        inv_w = consts[:, 145:149]
        inv_n = consts[:, 149:213].rearrange("p (g t c) -> p g t c", t=CH, c=2)
        dmask = consts[:, 213:229]

        ps = [psum("ps0"), psum("ps1")]
        psa = psum("psa")
        psb = psum("psb")
        xt = [psa, psb, ps[1]]

        def scratch(name, shape):
            return nc.dram_tensor(name, shape, F32).ap()

        coef_d = scratch("coef_d", [KT, P, GB * CF])
        k_d = scratch("k_d", [KT, P, GB * SG])
        u_d = scratch("u_d", [KT, P, SEQ])
        y_d = scratch("y_d", [KT, P, SEQ])
        yp_d = scratch("yp_d", [KT, P, SEQ])
        m1_d = scratch("m1_d", [KT, P, SEQ])
        gs_d = scratch("gs_d", [KT, P, SEQ])

        small_in = sem("small_in")
        ada_in = [sem(f"ada_in{q}") for q in range(KT)]
        tile_in = [sem(f"tile_in{n}") for n in range(KT)]
        raw_in = [sem("raw_in0"), sem("raw_in1")]
        raw_free = [sem("raw_free0"), sem("raw_free1")]
        hi_done, mm_done = sem("hi_done"), sem("mm_done")
        job_out = [sem("job_out0"), sem("job_out1")]
        c_in, silu_ready, mod_ready = sem("c_in"), sem("silu_ready"), sem("mod_ready")
        mod_prod, mod_sum, mod_acc_done = sem("mod_prod"), sem("mod_sum"), sem("mod_acc_done")
        xt_done, h_hi_done = sem("xt_done"), sem("h_hi_done")
        x_sums, x_var, x_root, x_scaled = sem("x_sums"), sem("x_var"), sem("x_root"), sem("x_scaled")
        h_full, h_done = sem("h_full"), sem("h_done")
        angle_ready, tabled = sem("angle_ready"), sem("tabled")
        turned, y_loaded = sem("turned"), sem("y_loaded")
        pw_in, pw_hi_done, pw_ready = sem("pw_in"), sem("pw_hi_done"), sem("pw_ready")
        dve_step, pool_step = sem("dve_step"), sem("pool_step")
        coef_ready, coef_stored, coef_in = sem("coef_ready"), sem("coef_stored"), sem("coef_in")
        pads_ready = sem("pads_ready")
        v_ready, tables_ready, wout_ready = sem("v_ready"), sem("tables_ready"), sem("wout_ready")
        a_done, win_ready, k_taken, k_ready = sem("a_done"), sem("win_ready"), sem("k_taken"), sem("k_ready")
        k_stored, toep_in, taps_ready = sem("k_stored"), sem("toep_in"), sem("taps_ready")
        u_stored, u_loaded = sem("u_stored"), sem("u_loaded")
        x_done, swapped, x_taken = sem("x_done"), sem("swapped"), sem("x_taken")
        z_ready, tables_used, sq_ready = sem("z_ready"), sem("tables_used"), sem("sq_ready")
        y_done, y_taken, y_stored = sem("y_done"), sem("y_taken"), sem("y_stored")
        pooled, pool_hi_done, pool_lo_done = sem("pooled"), sem("pool_hi_done"), sem("pool_lo_done")
        yp_stored = [sem("yp_stored0"), sem("yp_stored1")]
        gs_stored = [sem("gs_stored0"), sem("gs_stored1")]
        m1_stored = [sem("m1_stored0"), sem("m1_stored1")]
        in_hi_done, in_lo_done = sem("in_hi_done"), sem("in_lo_done")
        gate_taken, diag_ready, row_done, row_ready = (sem("gate_taken"), sem("diag_ready"),
                                                       sem("row_done"), sem("row_ready"))
        reload_in = [sem("reload_in0"), sem("reload_in1")]
        gated = sem("gated")
        g_in = [sem("g_in0"), sem("g_in1")]
        m_sum, m_hi_done, m_lo_done = sem("m_sum"), sem("m_hi_done"), sem("m_lo_done")
        o_sums, o_var, o_root, o_ready = sem("o_sums"), sem("o_var"), sem("o_root"), sem("o_ready")
        out_stored = [sem("out_stored0"), sem("out_stored1")]

        block = ctx.enter_context(nc.Block())

        def half(base, per, i, k):
            return (base + k) // 2 + (per // 2) * i

        x_view = x.rearrange("o (c t) d -> (o t) c d", t=CH)
        o_view = out.rearrange("o (c t) d -> (o t) c d", t=CH)

        def newton(steps, cols_, factor):
            tt, stt, ts = nc.vector.tensor_tensor, nc.vector.scalar_tensor_tensor, nc.vector.tensor_scalar
            var, root, r, t = stat[:, 1, cols_], stat[:, 2, cols_], stat[:, 3, cols_], stat[:, 4, cols_]
            steps.do(nc.vector.reciprocal(r, root))
            steps.do(tt(t, r, r, ALU.mult))
            steps.do(stt(t, t, -0.5, var, ALU.mult, ALU.mult))
            steps.do(stt(t, t, 1.5, r, ALU.add, ALU.mult))
            if factor != 1.0:
                steps.do(ts(t, t, factor, None, ALU.mult))

        MAGIC = 12582912.0
        names = ["are", "aim", "ldt", "dt", "f_re", "f_im", "den", "num", "t1", "t2", "t3", "t4"]
        par, off = {}, b_at
        for nme in names:
            par[nme] = at("par_" + nme, [P, G], off)[:, :]
            off += 4 * G
        wide = {}
        for nme in ["arg", "k", "r", "p", "q", "mag", "ang", "sn", "cs", "z", "cw", "sw2"]:
            wide[nme] = at("par_w_" + nme, [P, 2 * G], off)[:, :]
            off += 8 * G
        bits = at("par_bits", [P, 2 * G], off, I32)
        off += 8 * G
        pw_re, pw_im = at("pw_re", [P, G, 9], off), at("pw_im", [P, G, 9], off + 36 * G)
        off += 72 * G
        tmp_a, tmp_b = at("tmp_a", [P, G, 8], off), at("tmp_b", [P, G, 8], off + 32 * G)
        off += 64 * G
        tmp_c, tmp_d = at("tmp_c", [P, G, 8], off), at("tmp_d", [P, G, 8], off + 32 * G)
        off += 64 * G
        e_re, e_im = at("e_re", [P, 7, G], off), at("e_im", [P, 7, G], off + 28 * G)
        off += 56 * G
        assert off <= c_at

        def s5_steps(eng, steps):
            do, tt, ts = steps.do, eng.tensor_tensor, eng.tensor_scalar

            def cmul(o_re, o_im, a_re, a_im, b_re, b_im, t1, t2):
                steps.did(tt(t1, a_re, b_re, ALU.mult))
                steps.did(tt(t2, a_im, b_im, ALU.mult))
                steps.did(tt(o_re, a_re, b_im, ALU.mult))
                do(tt(o_im, a_im, b_re, ALU.mult))
                do(tt(o_im, o_im, o_re, ALU.add))
                do(tt(o_re, t1, t2, ALU.subtract))

            def square(o_re, o_im, a_re, a_im, t1, t2):
                steps.did(tt(t1, a_re, a_re, ALU.mult))
                steps.did(tt(t2, a_im, a_im, ALU.mult))
                do(tt(o_im, a_re, a_im, ALU.mult))
                steps.did(tt(o_re, t1, t2, ALU.subtract))
                do(tt(o_im, o_im, o_im, ALU.add))

            return do, tt, ts, cmul, square

        def rounded(steps, out_, in_, scale):
            steps.do(nc.vector.tensor_scalar(out_, in_, scale, MAGIC, ALU.mult, ALU.add))
            steps.do(nc.vector.tensor_scalar(out_, out_, MAGIC, None, ALU.subtract))

        def exp(steps, out_, in_, width):
            do = steps.do
            tt, stt, ts = nc.vector.tensor_tensor, nc.vector.scalar_tensor_tensor, nc.vector.tensor_scalar
            k, r, p, q = (wide[z][:, 0:width] for z in ("k", "r", "p", "q"))
            do(ts(q, in_, -87.0, 88.0, ALU.max, ALU.min))
            rounded(steps, k, q, 1.4426950408889634)
            do(stt(r, k, -0.693359375, q, ALU.mult, ALU.add))
            do(stt(r, k, 2.12194440054690583e-4, r, ALU.mult, ALU.add))
            c = [1.0, 1 / 2, 1 / 6, 1 / 24, 1 / 120, 1 / 720]
            do(ts(p, r, 1 / 5040, None, ALU.mult))
            for a in reversed(c):
                do(stt(p, p, a, r, ALU.add, ALU.mult))
            do(ts(p, p, 1.0, None, ALU.add))
            do(ts(bits[:, 0:width], k, 127.0, 8388608.0, ALU.add, ALU.mult))
            do(tt(p, p, bits[:, 0:width].bitcast(F32), ALU.mult))
            do(stt(out_, in_, -87.0, p, ALU.is_ge, ALU.mult))

        def plain_angles(steps):
            do, tt, ts = steps.do, nc.vector.tensor_tensor, nc.vector.tensor_scalar
            exp(steps, par["dt"], par["ldt"], G)
            do(tt(wide["ang"][:, 0:G], par["aim"], par["dt"], ALU.mult))
            do(ts(wide["ang"][:, G:], wide["ang"][:, 0:G], float(CH), None, ALU.mult))

        def magnitudes(steps):
            do, tt, ts = steps.do, nc.vector.tensor_tensor, nc.vector.tensor_scalar
            do(ts(par["are"], par["are"], -1e-4, None, ALU.min))
            do(tt(wide["arg"][:, 0:G], par["are"], par["dt"], ALU.mult))
            do(ts(wide["arg"][:, G:], wide["arg"][:, 0:G], float(CH), None, ALU.mult))
            exp(steps, wide["mag"], wide["arg"], 2 * G)
            do(nc.vector.tensor_copy(r8[:, :, :].rearrange("p b g -> p (b g)"), wide["mag"][:, G:]))

        def reduced_angles(steps):
            do, stt = steps.do, nc.vector.scalar_tensor_tensor
            k, r, q = (wide[m] for m in ("k", "r", "q"))
            src = wide["ang"]
            for scale in (2048.0, 1.0):
                rounded(steps, k, src, 1.0 / (1.5707963267948966 * scale))
                for part in half_pi_parts():
                    do(stt(r, k, -part * scale, src, ALU.mult, ALU.add))
                    src = r
            rounded(steps, q, k, 0.25)
            do(stt(q, q, -4.0, k, ALU.mult, ALU.add))

        def sine(steps):
            do = steps.do
            tt, stt, ts = nc.vector.tensor_tensor, nc.vector.scalar_tensor_tensor, nc.vector.tensor_scalar
            r, p, z = (wide[m] for m in ("r", "p", "z"))
            do(tt(z, r, r, ALU.mult))
            do(ts(p, z, 1 / 362880, -1 / 5040, ALU.mult, ALU.add))
            do(tt(p, p, z, ALU.mult))
            do(stt(p, p, 1 / 120, z, ALU.add, ALU.mult))
            do(stt(p, p, -1 / 6, z, ALU.add, ALU.mult))
            do(stt(wide["sn"], p, 1.0, r, ALU.add, ALU.mult))

        def cos_sin(steps):
            do = steps.do
            tt, stt, ts = nc.vector.tensor_tensor, nc.vector.scalar_tensor_tensor, nc.vector.tensor_scalar
            k, r, p, q, z = (wide[m] for m in ("k", "r", "p", "q", "z"))
            cs, sn = wide["cw"], wide["sw2"]
            do(ts(p, z, -1 / 3628800, 1 / 40320, ALU.mult, ALU.add))
            do(tt(p, p, z, ALU.mult))
            do(stt(p, p, -1 / 720, z, ALU.add, ALU.mult))
            do(stt(p, p, 1 / 24, z, ALU.add, ALU.mult))
            do(stt(p, p, -0.5, z, ALU.add, ALU.mult))
            do(ts(wide["cs"], p, 1.0, None, ALU.add))
            do(stt(p, q, -1.0, q, ALU.mult, ALU.max))
            do(ts(k, p, -1.0, 1.0, ALU.mult, ALU.add))
            do(ts(p, p, -1.0, 2.0, ALU.mult, ALU.add))
            do(tt(q, q, p, ALU.mult))
            do(tt(cs, k, wide["cs"], ALU.mult))
            do(tt(z, q, wide["sn"], ALU.mult))
            do(tt(cs, cs, z, ALU.subtract))
            do(tt(sn, k, wide["sn"], ALU.mult))
            do(tt(z, q, wide["cs"], ALU.mult))
            tt(sn, sn, z, ALU.add).then_inc(angle_ready, 1)

        def factors(steps):
            do, tt, ts = steps.do, nc.vector.tensor_tensor, nc.vector.tensor_scalar
            are, aim = par["are"], par["aim"]
            pr, pi = pw_re, pw_im
            do(nc.vector.memset(pr[:, :, 8:9], 1.0))
            do(nc.vector.memset(pi[:, :, 8:9], 0.0))
            do(tt(pr[:, :, 7], wide["mag"][:, 0:G], wide["cw"][:, 0:G], ALU.mult))
            do(tt(pi[:, :, 7], wide["mag"][:, 0:G], wide["sw2"][:, 0:G], ALU.mult))
            f_re, f_im, den, num = par["f_re"], par["f_im"], par["den"], par["num"]
            t1, t2 = par["t1"], par["t2"]
            do(tt(den, are, are, ALU.mult))
            do(tt(t1, aim, aim, ALU.mult))
            do(tt(den, den, t1, ALU.add))
            do(nc.vector.reciprocal(t2, den))
            do(ts(num, pr[:, :, 7], -1.0, None, ALU.add))
            do(tt(f_re, num, are, ALU.mult))
            do(tt(t1, pi[:, :, 7], aim, ALU.mult))
            do(tt(f_re, f_re, t1, ALU.add))
            do(tt(f_re, f_re, t2, ALU.mult))
            do(tt(f_im, pi[:, :, 7], are, ALU.mult))
            do(tt(t1, num, aim, ALU.mult))
            do(tt(f_im, f_im, t1, ALU.subtract))
            do(tt(f_im, f_im, t2, ALU.mult))

        def powers(steps):
            do, tt, ts, cmul, square = s5_steps(nc.vector, steps)
            pr, pi = pw_re, pw_im

            def power(dst, src, by, n):
                wideb = lambda a: a[:, :, by:by + 1].broadcast_to((P, G, n))
                cmul(pr[:, :, dst:dst + n], pi[:, :, dst:dst + n], pr[:, :, src:src + n], pi[:, :, src:src + n],
                     wideb(pr), wideb(pi), tmp_a[:, :, 0:n], tmp_b[:, :, 0:n])

            power(6, 7, 7, 1)
            power(4, 6, 6, 2)
            power(0, 4, 4, 4)

        def in_out_coefficients(steps):
            do, tt, ts, cmul, _ = s5_steps(nc.vector, steps)
            pr, pi, f_re, f_im = pw_re, pw_im, par["f_re"], par["f_im"]
            bf = lambda a: a.unsqueeze(2).broadcast_to((P, G, 8))
            cmul(coef[:, :, 0:8], coef[:, :, 8:16], pr[:, :, 1:9], pi[:, :, 1:9], bf(f_re), bf(f_im),
                 tmp_a[:, :, :], tmp_b[:, :, :])
            do(ts(coef[:, :, 8:16], coef[:, :, 8:16], sign, -1.0, ALU.mult, ALU.mult))
            do(ts(coef[:, :, 16:24], pr[:, :, 0:8], sign, None, ALU.mult))
            ts(coef[:, :, 24:32], pi[:, :, 0:8], -1.0, None, ALU.mult).then_inc(coef_ready, 1)

        def rotations(steps):
            do, tt, ts, cmul, square = s5_steps(nc.gpsimd, steps)
            t1, t2 = par["t3"], par["t4"]
            do(nc.gpsimd.tensor_copy(e_re[:, 0, :], wide["cw"][:, G:]))
            do(nc.gpsimd.tensor_copy(e_im[:, 0, :], wide["sw2"][:, G:]))
            for m in range(6):
                square(e_re[:, m + 1, :], e_im[:, m + 1, :], e_re[:, m, :], e_im[:, m, :], t1, t2)
            for at_re, at_im, first, levels in ((64, 80, 0, 4), (32, 40, 4, 3)):
                do(nc.gpsimd.memset(coef[:, :, at_re:at_re + 1], 1.0))
                do(nc.gpsimd.memset(coef[:, :, at_im:at_im + 1], 0.0))
                for l in range(levels):
                    n = 1 << l
                    er = e_re[:, first + l, :].unsqueeze(2).broadcast_to((P, G, n))
                    ei = e_im[:, first + l, :].unsqueeze(2).broadcast_to((P, G, n))
                    cmul(coef[:, :, at_re + n:at_re + 2 * n], coef[:, :, at_im + n:at_im + 2 * n],
                         coef[:, :, at_re:at_re + n], coef[:, :, at_im:at_im + n], er, ei,
                         tmp_c[:, :, 0:n], tmp_d[:, :, 0:n])

        def store_out(sp, t):
            parts = [slice(0, HALF), slice(HALF, D)] if t == CH - 1 else [slice(0, D)]
            for n, part in enumerate(parts):
                sp.wait_ge(o_ready, t + 1 + n)
                sp.dma_start(o_view[t][:, part], gt[t % 2][:, part]).then_inc(out_stored[t % 2], 16)

        @block.sync
        def _(sp):
            sp.sem_inc(k_stored, 16)
            sp.sem_inc(u_stored, 16)
            sp.sem_inc(y_stored, 16)
            for s in range(2):
                sp.sem_inc(yp_stored[s], 16)
                sp.sem_inc(m1_stored[s], 16)

            def load_w(w, before, slot, kt=KT):
                if before is not None:
                    sp.wait_ge(raw_free[slot], before)
                sp.dma_start(raw[slot][:, 0:kt, :], wstream_d[w][:, 0:kt, :]).then_inc(raw_in[slot], 16)

            def load_cf(b):
                sp.dma_start(cf[:, :, :], coef_d[b].rearrange("p (g f) -> p g f", f=CF)).then_inc(coef_in, 16)

            def load_bc(b):
                sp.dma_start(bc[:, :, :, :], bc_d[b].rearrange("p (q g h) -> p q g h", q=5, h=SG)).then_inc(coef_in, 16)

            sp.dma_start(cols[:, :], cols_d).then_inc(small_in, 16)
            sp.dma_start(consts[:, :], consts_d).then_inc(small_in, 16)
            sp.dma_start(silu_row[:, :], c_d).then_inc(c_in, 16)
            sp.dma_start(par["are"], a_re_d).then_inc(small_in, 16)
            sp.dma_start(par["aim"], a_im_d).then_inc(small_in, 16)
            sp.dma_start(par["ldt"], log_dt_d).then_inc(small_in, 16)
            for t in range(CH):
                sp.dma_start(x_tok[:, t, :], x_view[t]).then_inc(tile_in[t], 16)
            load_w(0, None, 0)
            load_w(1, None, 1)
            for k in range(KT):
                sp.dma_start(ada[:, :, k, :],
                             w_ada_d.rearrange("(s k) p m -> k p s m", s=2)[k]).then_inc(ada_in[k], 16)

            def next_w(w):
                load_w(w, w // 2, w % 2)

            sp.dma_start(pw_raw[:, :, :], pool_d[0]).then_inc(pw_in, 16)

            def store_gs(n, j, tile):
                sp.wait_ge(job_out[j % 2], j // 2 + 1)
                sp.dma_start(gs_d[n], tile[:, :]).then_inc(gs_stored[n % 2], 16)

            next_w(2)
            next_w(3)
            sp.wait_ge(h_done, KT)
            load_bc(0)
            next_w(4)
            store_gs(0, J_G, gt[0])
            next_w(5)
            store_gs(1, J_G + 1, gt[1])
            next_w(6)
            store_gs(2, J_G + 2, gt[0])
            sp.wait_ge(coef_ready, 3)
            sp.dma_start(coef_d.rearrange("b p f -> p b f"),
                         coef[:, :, :].rearrange("p (b g) f -> p b (g f)", g=GB)).then_inc(coef_stored, 16)
            store_gs(3, J_G + 3, gt[1])
            next_w(7)

            def store_u(b):
                sp.dma_start(u_d[b], u_out[:, :]).then_inc(u_stored, 16)

            def load_u(b):
                sp.wait_ge(y_done, b + 1)
                sp.wait_ge(u_stored, 16 * b + 32)
                src = u_d[b].rearrange("(g h) (t c) -> t h g c", h=SG, t=CH)
                for t in range(CH):
                    sp.dma_start(u_in[SG * t:SG * t + SG, :, :], src[t]).then_inc(u_loaded, 16)

            def kernel_taps(b):
                sp.wait_ge(k_ready, b + 1)
                sp.dma_start(k_d[b], ks[:, :, :].rearrange("p g h -> p (g h)")).then_inc(k_stored, 16)
                sp.wait_ge(k_stored, 16 * b + 32)
                src = k_d[b].rearrange("(j h) x -> h j x", h=SG)
                for t in range(CH):
                    sp.dma_start(toep[SG * t:SG * t + SG, 0:CH - t, :, :].rearrange("p r g h -> p r (g h)"),
                                 src[:, t:CH, :]).then_inc(toep_in, 16)

            def store_y(b):
                sp.wait_ge(y_taken, b + 2)
                dst = y_d[b].rearrange("(g h) (t c) -> t h g c", h=SG, t=CH)
                for r in range(CH):
                    sp.dma_start(dst[CH - 1 - r], y_act[SG * r:SG * r + SG, :, :]).then_inc(y_stored, 16)

            def store_yp(i, q):
                sp.wait_ge(job_out[1 - q], half(J_P, 8, i, 6 + q) + 1)
                sp.dma_start(yp_d[2 * i + q], rt[q][:, :]).then_inc(yp_stored[q], 16)

            sp.wait_ge(job_out[0], (J_P - 1) // 2 + 1)
            store_u(0)
            load_u(0)

            def turn1(i, last):
                n = 2 * i

                def w(k):
                    load_w(W_P + 6 * i + k, half(W_P, 6, i, k), (W_P + k) % 2)

                w(3)
                w(4)
                kernel_taps(n)
                sp.wait_ge(wout_ready, n + 1)
                load_cf(n + 1)
                load_bc(n + 1)
                w(5)
                sp.wait_ge(job_out[1], half(J_P, 8, i, 2) + 1)
                store_u(n + 1)
                w(6)
                load_u(n + 1)
                store_y(n)
                w(7)
                kernel_taps(n + 1)
                sp.wait_ge(wout_ready, n + 2)
                if not last:
                    load_cf(n + 2)
                    load_bc(n + 2)
                w(8)
                if not last:
                    sp.wait_ge(pw_ready, i + 1)
                    sp.dma_start(pw_raw[:, :, :], pool_d[i + 1]).then_inc(pw_in, 16)
                    sp.wait_ge(job_out[0], half(J_P, 8, i, 5) + 1)
                    store_u(n + 2)
                    load_u(n + 2)
                    store_y(n + 1)
                    store_yp(i, 0)
                    store_yp(i, 1)

            with sp.Fori(0, 3) as i:
                turn1(i, False)
            turn1(3, True)

            def load_yp(n):
                sp.dma_start(in_raw[:, n, :], yp_d[n]).then_inc(tile_in[n], 16)

            store_gs(4, J_F1 - 3, u_out)
            sp.wait_ge(pool_lo_done, KT)
            sp.wait_ge(yp_stored[0], 16 * 4)
            sp.wait_ge(yp_stored[1], 16 * 4)
            load_yp(0)
            load_yp(1)
            store_y(KT - 1)
            sp.wait_ge(mm_done, J_F1)
            for n in range(2, 6):
                load_yp(n)
            for q in range(2):
                store_yp(3, q)
            for q in range(2):
                sp.wait_ge(yp_stored[q], 16 * 5)
                load_yp(6 + q)
            sp.dma_start(silu_row[:, :], c_d).then_inc(c_in, 16)
            next_w(W_BP + 2)
            store_gs(5, J_F1, gt[1])
            sp.wait_ge(y_stored, 16 * CH * KT + 16)
            sp.wait_ge(gs_stored[0], 16 * 3)
            for n in range(KT):
                sp.dma_start(y_raw[:, n, :], y_d[n]).then_inc(y_loaded, 16)
            with sp.Fori(0, 4) as i:
                for k in range(6):
                    w = k + 3
                    load_w(W_BP + 6 * i + w, half(W_BP, 6, i, w), w % 2)
                    if k in (1, 5):
                        q = k // 4
                        sp.wait_ge(job_out[1], half(J_BP, 4, i, 2 * q + 1) + 1)
                        sp.dma_start(m1_d[2 * i + q], rt[q][:, :]).then_inc(m1_stored[q], 16)
            sp.wait_ge(m1_stored[0], 16 * 5)
            sp.wait_ge(m1_stored[1], 16 * 5)
            for q in range(2):
                sp.dma_start(rt[q][:, :], y_d[q]).then_inc(reload_in[q], 16)

            def turn3(i, last):
                for k in range(4):
                    w = k + 3
                    load_w(W_GLU + 4 * i + w, half(W_GLU, 4, i, w), w % 2)
                    if k in (1, 3) and not last:
                        q = k // 2
                        sp.wait_ge(gated, 2 * i + q + 3)
                        sp.dma_start(rt[q][:, :], y_d[2 * i + q + 2]).then_inc(reload_in[q], 16)

            with sp.Fori(0, 3) as i:
                turn3(i, False)
            turn3(3, True)
            sp.wait_ge(mm_done, J_F3)
            sp.wait_ge(gated, KT + 2)
            for n in range(KT):
                sp.dma_start(wo_raw[:, n, :], w_out_d[n * P:n * P + P, :]).then_inc(tile_in[n], 16)
            for n in range(2):
                sp.dma_start(rt[n][:, :], m1_d[n]).then_inc(reload_in[n], 16)
            for q in range(2):
                next_w(W_F3 + q + 3)
                store_gs(6 + q, J_F3 + q, gt[q])
            for s in range(2):
                sp.wait_ge(gs_stored[s], 16 * 4)
                sp.dma_start(gt[s][:, :], gs_d[s]).then_inc(g_in[s], 16)
            for n in range(KT):
                if W_BS + n + 3 < W_ALL:
                    next_w(W_BS + n + 3)
                sp.wait_ge(m_lo_done, n + 1)
                if n + 2 < KT:
                    sp.dma_start(rt[n % 2][:, :], m1_d[n + 2]).then_inc(reload_in[n % 2], 16)
                    sp.dma_start(gt[n % 2][:, :], gs_d[n + 2]).then_inc(g_in[n % 2], 16)
            for t in range(CH):
                if t >= 2:
                    store_out(sp, t - 2)
                sp.dma_start(rt[t % 2][:, :], x_view[t]).then_inc(reload_in[t % 2], 16)
            for t in range(CH - 2, CH):
                store_out(sp, t)
            for s in range(2):
                sp.wait_ge(out_stored[s], 16 * (4 + s))

        @block.gpsimd
        def _(pool):
            steps = Steps(pool, pool_step)
            tt = nc.gpsimd.tensor_tensor

            def bcast(ap, axis, n):
                shape = list(ap.shape)
                shape.insert(axis, n)
                return ap.unsqueeze(axis).broadcast_to(tuple(shape))

            def batch(b):
                pool.wait_ge(coef_in, 32 * b + 32)
                pool.wait_ge(a_done, b + 1)
                steps.did(tt(vt[:, :, :, :], bcast(cf[:, :, 8:16], 3, SG), bcast(bc[:, 1, :, :], 2, CH), ALU.mult))
                steps.did(nc.gpsimd.tensor_scalar(cc[:, :, :], bc[:, 2, :, :], sign, None, ALU.mult))
                steps.do(tt(v[:, :, :, :], bcast(cf[:, :, 0:8], 3, SG), bcast(bc[:, 0, :, :], 2, CH), ALU.mult))
                tt(v[:, :, :, :], v[:, :, :, :], vt[:, :, :, :], ALU.add).then_inc(v_ready, 1)
                ear, eai = cf[:, :, 32:40], cf[:, :, 40:48]
                sai, sar = cf[:, :, 48:56], cf[:, :, 56:64]
                ebr, ebi = cf[:, :, 64:80], cf[:, :, 80:96]
                cos4 = cos_t[:, :, :].rearrange("p g (a b) -> p g a b", b=16)
                sin4 = sin_t[:, :, :].rearrange("p g (a b) -> p g a b", b=16)
                vt4 = vt[:, :, :, :]
                pool.wait_ge(v_ready, b + 1)
                pool.wait_ge(tables_used, b + 1)
                steps.did(tt(cos4, bcast(ear, 3, 16), bcast(ebr, 2, 8), ALU.mult))
                steps.do(tt(vt4, bcast(eai, 3, 16), bcast(ebi, 2, 8), ALU.mult))
                steps.do(tt(cos4, cos4, vt4, ALU.subtract))
                steps.did(tt(sin4, bcast(sai, 3, 16), bcast(ebr, 2, 8), ALU.mult))
                steps.do(tt(vt4, bcast(sar, 3, 16), bcast(ebi, 2, 8), ALU.mult))
                tt(sin4, sin4, vt4, ALU.add).then_inc(tables_ready, 1)
                pool.wait_ge(tables_ready, b + 1)
                pool.wait_ge(y_done, b + 1)
                steps.did(tt(vt4, bcast(cf[:, :, 24:32], 3, SG), bcast(bc[:, 3, :, :], 2, CH), ALU.mult))
                steps.do(tt(wout[:, :, :, :], bcast(cf[:, :, 16:24], 3, SG), bcast(bc[:, 2, :, :], 2, CH), ALU.mult))
                tt(wout[:, :, :, :], wout[:, :, :, :], vt4, ALU.add).then_inc(wout_ready, 1)
                pool.wait_ge(wout_ready, b + 1)

            pool.wait_ge(silu_ready, 1)
            for k in range(KT):
                pool.wait_ge(ada_in[k], 16)
                if k >= 2:
                    pool.wait_ge(mod_sum, k - 1)
                tt(rt[k % 2][:, :], ada[:, 0, k, :], silu_row[:, :], ALU.mult).then_inc(mod_prod, 1)
            pool.wait_ge(angle_ready, 1)
            rotations(steps)
            pool.sem_inc(tabled, 1)
            with pool.Fori(0, KT) as b:
                steps.loop(b, 10)
                batch(b)
            steps.end(KT)

        @block.scalar
        def _(act):
            fn = nc.scalar.activation

            def split_hi(before, slot, after=None):
                act.wait_ge(raw_in[slot], 16 * before + 16)
                if after is not None:
                    act.wait_ge(mm_done, after + 1)
                fn(w_hi[slot][:, :, :], raw[slot][:, :, :], ACT.Copy).then_inc(hi_done, 1)

            act.wait_ge(c_in, 16)
            fn(silu_row[:, :], silu_row[:, :], ACT.Silu).then_inc(silu_ready, 1)
            act.wait_ge(small_in, 16 * 5)
            fn(glub[:, :], glu_b, ACT.Copy, scale=0.5)
            for half_ in range(2):
                for t in range(4 * half_, 4 * half_ + 4):
                    act.wait_ge(tile_in[t], 16)
                    if t:
                        act.wait_ge(x_sums, t)
                    fn(gt[t % 2][:, :], x_tok[:, t, :], ACT.Square, accum_out=stat[:, 0, t:t + 1]).then_inc(x_sums, 1)
                act.wait_ge(x_var, half_ + 1)
                cols4 = slice(4 * half_, 4 * half_ + 4)
                fn(stat[:, 2, cols4], stat[:, 1, cols4], ACT.Sqrt).then_inc(x_root, 1)
            split_hi(0, 0)
            split_hi(0, 1)
            def shift_sum(k):
                act.wait_ge(mod_prod, k + 1)
                fn(rt[k % 2][:, :], rt[k % 2][:, :], ACT.Copy, accum_out=mod_acc[:, k:k + 1]).then_inc(mod_sum, 1)

            shift_sum(0)
            for k in range(KT):
                if k < KT - 1:
                    shift_sum(k + 1)
                act.wait_ge(xt_done, k + 1)
                act.wait_ge(mod_ready, 2 * k + 2)
                if k >= 2:
                    act.wait_ge(h_done, k - 1)
                fn(gt[k % 2][:, :], xt[k % 3][:, :], ACT.Identity, bias=s_col[:, k:k + 1],
                   scale=g_col[:, k:k + 1]).then_inc(h_full, 1)
                if k in ACT_HIGH:
                    act.wait_ge(h_full, k + 1)
                    fn(h_hi[:, k, :], gt[k % 2][:, :], ACT.Copy).then_inc(h_hi_done, 1)
            act.wait_ge(h_done, KT)

            def evac(j, slot, dst, func, **kw):
                act.wait_ge(mm_done, j + 1)
                src = ps[slot][:, :]
                if len(dst.shape) == 3:
                    src = src.rearrange("p (t c) -> p t c", c=NC)
                fn(dst, src, func, **kw).then_inc(job_out[slot], 1)

            def gate_job(j, dst):
                evac(j, j % 2, dst[:, :], ACT.Tanh, scale=0.5)

            for q in range(4):
                if q >= 2:
                    act.wait_ge(gs_stored[q % 2], 16)
                gate_job(J_G + q, gt[q % 2])
                split_hi((q + 2) // 2, q % 2, J_G + q)
            act.wait_ge(pads_ready, 5)

            def win_out(b):
                act.wait_ge(turned, b + 1)
                fn(win[:, :, :].rearrange("p g q -> p (g q)"), psa[:, :], ACT.Copy).then_inc(win_ready, 1)

            def taps_out(b):
                act.wait_ge(a_done, b + 2)
                act.wait_ge(k_stored, 16 * b + 16)
                fn(ks[:, :, :].rearrange("p g h -> p (g h)"), psb[:, 0:P], ACT.Copy).then_inc(k_taken, 1)

            def swap_x(b):
                act.wait_ge(x_done, b + 1)
                sw2 = sw[:, :, :].rearrange("p g c -> p (g c)")
                fn(sw2[0:NS, :], psa[NS:P, :], ACT.Copy)
                fn(sw2[NS:P, :], psa[0:NS, :], ACT.Copy).then_inc(swapped, 1)

            def order_taps(b):
                act.wait_ge(toep_in, 16 * CH * b + 16 * CH)
                act.wait_ge(y_done, b + 1)
                fn(taps[:, :, :, :], toep[:, :, :, :].rearrange("p r g h -> p g r h"), ACT.Copy).then_inc(taps_ready, 1)

            def swap_z(b):
                act.wait_ge(z_ready, b + 1)
                fn(sw[0:NS, :, :], st[NS:P, :, :], ACT.Copy)
                fn(sw[NS:P, :, :], st[0:NS, :, :], ACT.Copy).then_inc(swapped, 1)

            def y_out(b):
                act.wait_ge(y_done, b + 2)
                act.wait_ge(y_stored, 16 * CH * b + 16)
                fn(y_act[:, :, :].rearrange("p g c -> p (g c)"), psb[:, :], ACT.Gelu_apprx_tanh).then_inc(y_taken, 1)

            def pool_high(n, q, i):
                act.wait_ge(pooled, n + 2)
                if q == 0:
                    act.wait_ge(mm_done, 8 * i + J_P)
                fn(pool_hi[:, q, :].rearrange("p (t c) -> p t c", c=NC), pa[:, :, 1:NC + 1], ACT.Copy).then_inc(pool_hi_done, 1)

            evac(J_P - 1, 0, u_out[:, :], ACT.Copy)
            split_hi(3, 0, J_P - 1)
            win_out(0)
            for s in range(2):
                act.wait_ge(gs_stored[s], 32)

            def turn1(i, last):
                n = 2 * i

                def hi(k):
                    split_hi(half(W_P, 6, i, k), (W_P + k) % 2, J_P + 8 * i + k - 2)

                def out(k, dst, func):
                    evac(J_P + 8 * i + k, (J_P + k) % 2, dst, func)

                def states(b):
                    taps_out(b)
                    swap_x(b)
                    swap_z(b)
                    order_taps(b)

                act.wait_ge(pooled, n + 1)
                out(0, pu[:, :, 1:NC + 1], ACT.Copy)
                hi(2)
                states(n)
                out(1, gt[0][:, :], ACT.Silu)
                hi(3)
                act.wait_ge(u_stored, 16 * n + 32)
                out(2, u_out[:, :], ACT.Copy)
                pool_high(n, 0, i)
                hi(4)
                y_out(n)
                win_out(n + 1)
                act.wait_ge(pooled, n + 2)
                out(3, pu[:, :, 1:NC + 1], ACT.Copy)
                hi(5)
                act.wait_ge(pw_in, 16 * i + 16)
                act.wait_ge(mm_done, J_P + 8 * i)
                fn(pw_hi[:, :, :], pw_raw[:, :, :], ACT.Copy).then_inc(pw_hi_done, 1)
                states(n + 1)
                out(4, gt[1][:, :], ACT.Silu)
                hi(6)
                act.wait_ge(u_stored, 16 * n + 48)
                if last:
                    gate_job(J_F1 - 3, u_out)
                else:
                    out(5, u_out[:, :], ACT.Copy)
                hi(7)
                pool_high(n + 1, 1, i)
                y_out(n + 1)
                if not last:
                    win_out(n + 2)

            with act.Fori(0, 3) as i:
                turn1(i, False)
            turn1(3, True)

            def hi_at(w, after):
                split_hi(w // 2, w % 2, after)

            act.wait_ge(mm_done, J_F1)
            for n in range(KT):
                if n == 6:
                    act.wait_ge(job_out[0], (J_F1 - 1) // 2 + 1)
                    gate_job(J_F1, gt[1])
                act.wait_ge(tile_in[n], 32)
                fn(in_hi[:, n, :], in_raw[:, n, :], ACT.Copy).then_inc(in_hi_done, 1)
            act.wait_ge(c_in, 32)
            fn(silu_row[:, :], silu_row[:, :], ACT.Silu).then_inc(silu_ready, 1)
            act.wait_ge(gs_stored[1], 16 * 3)
            with act.Fori(0, 4) as i:
                def hi2(k, w=None):
                    w = k if w is None else w
                    split_hi(half(W_BP, 6, i, w), k % 2, J_BP + 4 * i + k - 2)

                hi2(1)
                evac(J_BP + 4 * i, 0, gt[0][:, :], ACT.Tanh, scale=0.5)
                hi2(2)
                hi2(3, 5)
                evac(J_BP + 4 * i + 2, 0, gt[1][:, :], ACT.Tanh, scale=0.5)
                hi2(4, 6)
            act.wait_ge(mm_done, J_GLU)
            act.wait_ge(y_loaded, 16 * KT)
            for n in range(KT):
                fn(in_hi[:, n, :], y_raw[:, n, :], ACT.Copy).then_inc(in_hi_done, 1)
                if n == 2:
                    hi_at(W_GLU + 1, J_GLU - 1)
            with act.Fori(0, 4) as i:
                def hi3(k):
                    split_hi(half(W_GLU, 4, i, k), k % 2, J_GLU + 4 * i + k - 2)

                for q in range(2):
                    n = 2 * i + q
                    act.wait_ge(gated, n + 1)
                    evac(J_GLU + 4 * i + 2 * q, 0, gt[q][:, :], ACT.Silu)
                    hi3(2 * q + 2)
                    evac(J_GLU + 4 * i + 2 * q + 1, 1, ys_raw[:, n, :], ACT.Tanh, scale=0.5,
                         bias=glub[:, bass.ds(n, 1)])
                    hi3(2 * q + 3)
            act.wait_ge(gated, KT + 2)
            for n in range(KT):
                fn(in_hi[:, n, :], ys_raw[:, n, :], ACT.Copy).then_inc(in_hi_done, 1)
            for q in range(2):
                gate_job(J_F3 + q, gt[q])
                if q == 0:
                    hi_at(W_BS, J_F3)
            act.wait_ge(row_done, 1)
            fn(gate_row[:, :], psa[:, :], ACT.Copy).then_inc(row_ready, 1)

            def m_high(n, q):
                act.wait_ge(m_sum, n + 1)
                fn(m_hi[:, n, :], rt[q][:, :], ACT.Copy).then_inc(m_hi_done, 1)

            def wo_high(n):
                act.wait_ge(tile_in[n], 16 * 3)
                fn(wo_hi[n], wo_raw[:, n, :], ACT.Copy).then_inc(in_hi_done, 1)

            def turn4(i, last):
                for q in range(2):
                    if last and q == 1:
                        act.wait_ge(mm_done, J_OUT - 1)
                        act.wait_ge(raw_free[1], W_ALL // 2)
                        for n in range(3):
                            wo_high(n)
                        act.wait_ge(mm_done, J_OUT)
                        wo_high(3)
                        wo_high(4)
                    else:
                        split_hi(half(W_BS, 2, i, q + 1), (q + 1) % 2, J_BS + 2 * i + q - 1)
                    m_high(2 * i + q, q)

            with act.Fori(0, 3) as i:
                turn4(i, False)
            turn4(3, True)
            for n in range(5, KT):
                wo_high(n)
            for t in range(CH):
                if t:
                    act.wait_ge(o_sums, t)
                if t < CH - 1:
                    act.wait_ge(mm_done, J_OUT + t + 1)
                    fn(squares[:, :], ps[t % 2][:, :], ACT.Square, accum_out=stat[:, 0, t:t + 1]).then_inc(o_sums, 1)
                else:
                    for f in range(2):
                        act.wait_ge(mm_done, J_OUT + t + 1 + f)
                        fn(squares[:, f * HALF:f * HALF + HALF], ps[t % 2][:, f * HALF:f * HALF + HALF], ACT.Square,
                           accum_out=stat[:, 5 * f, t:t + 1]).then_inc(o_sums, 1)
                act.wait_ge(o_var, t + 1)
                fn(stat[:, 2, t:t + 1], stat[:, 1, t:t + 1], ACT.Sqrt).then_inc(o_root, 1)

        @block.vector
        def _(dve):
            tt, stt = nc.vector.tensor_tensor, nc.vector.scalar_tensor_tensor
            ts = nc.vector.tensor_scalar
            steps = Steps(dve, dve_step)
            do, did = steps.do, steps.did

            def split_lo(nth, slot):
                dve.wait_ge(hi_done, nth)
                tt(w_lo[slot][:, :, :], raw[slot][:, :, :], w_hi[slot][:, :, :].bitcast(F32),
                   ALU.subtract).then_inc(raw_free[slot], 1)

            def row_sum(scratch_, row, acc):
                return stt(scratch_, row, 1.0, silu_row[:, :], ALU.mult, ALU.mult, accum_out=acc)

            dve.wait_ge(small_in, 16 * 5)
            plain_angles(steps)
            reduced_angles(steps)
            for half_ in range(2):
                cols4 = slice(4 * half_, 4 * half_ + 4)
                dve.wait_ge(x_sums, 4 * half_ + 4)
                ts(stat[:, 1, cols4], stat[:, 0, cols4], 1.0 / D, EPS, ALU.mult, ALU.add).then_inc(x_var, 1)
                dve.wait_ge(x_root, half_ + 1)
                newton(steps, cols4, 1.0)
                for t in range(4 * half_, 4 * half_ + 4):
                    ts(diag[:, t, :], ident, stat[:, 4, t:t + 1], None, ALU.mult).then_inc(x_scaled, 1)
                if half_ == 0:
                    sine(steps)
            cos_sin(steps)
            split_lo(1, 0)
            dve.wait_ge(silu_ready, 1)
            ts(g_col[:, :], b_ada[:, KT:2 * KT], 1.0, None, ALU.add).then_inc(mod_acc_done, 1)

            def scale_shift(k):
                dve.wait_ge(ada_in[k], 16)
                row_sum(mod_out[:, k % 2, :], ada[:, 1, k, :], mod_acc[:, KT + k:KT + k + 1]).then_inc(mod_acc_done, 1)
                dve.wait_ge(mod_acc_done, k + 2)
                stt(g_col[:, k:k + 1], mod_acc[:, KT + k:KT + k + 1], g_col[:, k:k + 1], npre[:, k:k + 1],
                    ALU.add, ALU.mult).then_inc(mod_ready, 1)
                dve.wait_ge(mod_sum, k + 1)
                tt(s_col[:, k:k + 1], mod_acc[:, k:k + 1], b_ada[:, k:k + 1], ALU.add).then_inc(mod_ready, 1)

            def split_h(k):
                if k in ACT_HIGH:
                    dve.wait_ge(h_hi_done, ACT_HIGH.index(k) + 1)
                else:
                    dve.wait_ge(h_full, k + 1)
                    do(nc.vector.tensor_copy(h_hi[:, k, :], gt[k % 2][:, :]))
                tt(h_lo[:, k, :], gt[k % 2][:, :], h_hi[:, k, :].bitcast(F32), ALU.subtract).then_inc(h_done, 1)

            for k in range(KT):
                scale_shift(k)
                if k:
                    split_h(k - 1)
            split_h(KT - 1)
            split_lo(2, 1)
            dve.sem_inc(y_taken, 1)
            magnitudes(steps)
            split_lo(3, 0)
            dve.wait_ge(angle_ready, 1)
            factors(steps)
            powers(steps)
            split_lo(4, 1)
            in_out_coefficients(steps)
            split_lo(5, 0)
            dve.wait_ge(tabled, 1)
            ts(coef[:, :, 48:56], coef[:, :, 40:48], sign, None, ALU.mult).then_inc(coef_ready, 1)
            ts(coef[:, :, 56:64], coef[:, :, 32:40], sign, None, ALU.mult).then_inc(coef_ready, 1)
            dve.wait_ge(coef_ready, 3)
            dve.wait_ge(h_done, KT)
            dve.wait_ge(xt_done, KT)
            nc.vector.tensor_copy(cf[:, :, :], coef[:, 0:GB, :]).then_inc(coef_in, 16)
            dve.wait_ge(coef_stored, 16)
            dve.wait_ge(coef_in, 32)
            nc.vector.memset(toep[:, :, :, :], 0.0).then_inc(pads_ready, 1)
            nc.vector.memset(sq[:, :, 0:1], 0.0).then_inc(pads_ready, 1)
            for z in (pu, pa, pb):
                nc.vector.memset(z[:, :, 0:1], 0.0).then_inc(pads_ready, 1)
            dve.wait_ge(pads_ready, 5)
            dve.sem_inc(pooled, 1)
            dve.sem_inc(tables_used, 1)
            dve.sem_inc(x_taken, 1)
            split_lo(6, 1)
            split_lo(7, 0)

            def d_skip(b):
                dve.wait_ge(k_taken, b + 1)
                do(tt(dk[96:P, :, :], bc[96:P, 4, :, :], dmask[96:P, :].unsqueeze(1).broadcast_to((32, GB, SG)),
                      ALU.mult))
                tt(ks[96:P, :, :], ks[96:P, :, :], dk[96:P, :, :], ALU.add).then_inc(k_ready, 1)

            def rotate_in(b):
                flat = lambda a: a[:, :, :].rearrange("p g c -> p (g c)")
                dve.wait_ge(tables_ready, b + 1)
                dve.wait_ge(swapped, 2 * b + 1)
                did(tt(flat(sw), flat(sw), flat(sin_t), ALU.mult))
                tt(flat(st), psa[:, :], flat(cos_t), ALU.mult).then_inc(x_taken, 1)
                dve.wait_ge(x_taken, b + 2)
                steps.landed()
                do(tt(flat(st), flat(st), flat(sw), ALU.add))
                for g in range(GB):
                    ins = nc.vector.tensor_tensor_scan(st[:, g, :], r8[:, b, g:g + 1].broadcast_to((P, NC)),
                                                       st[:, g, :], 0.0, ALU.mult, ALU.add)
                    if g < GB - 1:
                        did(ins)
                ins.then_inc(z_ready, 1)

            def rotate_out(b):
                flat = lambda a: a[:, :, :].rearrange("p g c -> p (g c)")
                dve.wait_ge(swapped, 2 * b + 2)
                did(tt(flat(sw), flat(sw), flat(sin_t), ALU.mult))
                tt(flat(st), flat(st), flat(cos_t), ALU.mult).then_inc(tables_used, 1)
                dve.wait_ge(tables_used, b + 2)
                steps.landed()
                tt(sq[:, :, 1:NC], st[:, :, 0:NC - 1], sw[:, :, 0:NC - 1], ALU.subtract).then_inc(sq_ready, 1)

            def pooling(n, q, i, slot, jk):
                dve.wait_ge(job_out[slot], half(J_P, 8, i, jk) + 1)
                bufs = [pu, pa, pb, pa, pb]
                for l in range(LEVELS):
                    s, o, d = bufs[l], bufs[l + 1], 1 << l
                    on = level_on[:, i, l:l + 1]
                    if d < CH:
                        did(stt(o[:, d:CH, 1:NC + 1], s[:, 0:CH - d, 1:NC + 1], on, s[:, d:CH, 1:NC + 1],
                                ALU.mult, ALU.add))
                    do(stt(o[:, 0:d, 1:NC + 1], s[:, CH - d:CH, 0:NC], on, s[:, 0:d, 1:NC + 1],
                           ALU.mult, ALU.add))
                did(stt(pa[:, :, 1:NC + 1], pb[:, :, 1:NC + 1], inv_w[:, bass.ds(i, 1)], pu[:, :, 1:NC + 1],
                        ALU.mult, ALU.subtract))
                do(tt(pfix[:, :, :], pb[:, :, 1:3], inv_n[:, i, :, :], ALU.mult))
                tt(pa[:, :, 1:3], pfix[:, :, :], pu[:, :, 1:3], ALU.subtract).then_inc(pooled, 1)
                dve.wait_ge(pool_hi_done, n + 1)
                tt(pool_lo[:, q, :].rearrange("p (t c) -> p t c", c=NC), pa[:, :, 1:NC + 1],
                   pool_hi[:, q, :].bitcast(F32).rearrange("p (t c) -> p t c", c=NC),
                   ALU.subtract).then_inc(pool_lo_done, 1)

            def yp_out(i, q):
                slot = 1 - q
                dve.wait_ge(mm_done, J_P + 8 * i + 6 + q + 1)
                dve.wait_ge(yp_stored[q], 16 * i + 16)
                stt(rt[q][:, :], ps[slot][:, :], pscale[:, bass.ds(2 * i + q, 1)], gt[q][:, :],
                    ALU.mult, ALU.mult).then_inc(job_out[slot], 1)

            def pool_weights_low(i):
                dve.wait_ge(pw_hi_done, i + 1)
                tt(pw_lo[:, :, :], pw_raw[:, :, :], pw_hi[:, :, :].bitcast(F32), ALU.subtract).then_inc(pw_ready, 1)

            with dve.Fori(0, 4) as i:
                steps.loop(i, 40)
                n = 2 * i

                def lo(k):
                    split_lo(W_P + 6 * i + k + 1, (W_P + k) % 2)

                lo(2)
                d_skip(n)
                rotate_in(n)
                rotate_out(n)
                lo(3)
                pooling(n, 0, i, 1, 0)
                lo(4)
                lo(5)
                d_skip(n + 1)
                pool_weights_low(i)
                rotate_in(n + 1)
                rotate_out(n + 1)
                lo(6)
                pooling(n + 1, 1, i, 0, 3)
                lo(7)
                yp_out(i, 0)
                yp_out(i, 1)
            steps.end(4)

            for n in range(KT):
                dve.wait_ge(in_hi_done, n + 1)
                tt(in_lo[:, n, :], in_raw[:, n, :], in_hi[:, n, :].bitcast(F32), ALU.subtract).then_inc(in_lo_done, 1)
            dve.wait_ge(silu_ready, 2)
            with dve.Fori(0, 4) as i:
                def lo2(k):
                    split_lo(4 * i + J_BP + k - 7, k % 2)

                def m1_out(q):
                    k = 2 * q + 1
                    dve.wait_ge(job_out[0], half(J_BP, 4, i, 2 * q) + 1)
                    dve.wait_ge(mm_done, 4 * i + J_BP + k + 1)
                    dve.wait_ge(m1_stored[q], 16 * i + 16)
                    stt(rt[q][:, :], gt[q][:, :], 1.0, ps[1][:, :], ALU.add, ALU.mult).then_inc(job_out[1], 1)

                lo2(1)
                lo2(2)
                m1_out(0)
                for q in range(2):
                    dve.wait_ge(raw_in[1 - q], 16 * half(W_BP, 6, i, 3 + q) + 16)
                    row_sum((psa, psb)[q][:, :], raw[1 - q][:, :, :].rearrange("p k m -> p (k m)"),
                            mod_acc[:, q:q + 1]).then_inc(raw_free[1 - q], 1)
                for q in range(2):
                    dve.wait_ge(raw_free[1 - q], half(W_BP, 6, i, 3 + q) + 1)
                    stt(gate_col[:, bass.ds(2 * i + q, 1)], mod_acc[:, q:q + 1], b_ada[:, bass.ds(2 * i + q + 16, 1)],
                        npost[:, bass.ds(2 * i + q, 1)], ALU.add, ALU.mult).then_inc(gate_taken, 1)
                lo2(3)
                lo2(4)
                m1_out(1)
                dve.wait_ge(gate_taken, 2 * i + 2)
            for n in range(KT):
                dve.wait_ge(in_hi_done, KT + n + 1)
                tt(in_lo[:, n, :], y_raw[:, n, :], in_hi[:, n, :].bitcast(F32), ALU.subtract).then_inc(in_lo_done, 1)
                if n == 2:
                    split_lo(J_GLU + 1 - 7, 1)
            dve.wait_ge(gate_taken, KT)
            nc.vector.memset(ones[:, :], 1.0).then_inc(diag_ready, 1)
            for k in range(KT):
                ts(gate_row[:, k * P:k * P + P], ident, gate_col[:, k:k + 1], None, ALU.mult).then_inc(diag_ready, 1)
            dve.sem_inc(gated, 2)
            with dve.Fori(0, 4) as i:
                steps.loop(i, 2)

                def lo3(k):
                    split_lo(4 * i + J_GLU + k - 7, k % 2)

                for q in range(2):
                    n = 2 * i + q
                    lo3(2 * q + 2)
                    dve.wait_ge(reload_in[q], 16 * i + 16)
                    dve.wait_ge(job_out[0], half(J_GLU, 4, i, 2 * q) + 1)
                    dve.wait_ge(job_out[1], half(J_GLU, 4, i, 2 * q + 1) + 1)
                    do(stt(ys_raw[:, n, :], ys_raw[:, n, :], 1.0, rt[q][:, :], ALU.add, ALU.mult))
                    stt(ys_raw[:, n, :], ys_raw[:, n, :], 0.5, gt[q][:, :], ALU.mult, ALU.mult).then_inc(gated, 1)
                    lo3(2 * q + 3)
            steps.end(4)
            for n in range(KT):
                dve.wait_ge(in_hi_done, 2 * KT + n + 1)
                tt(ys_lo[:, n, :], ys_raw[:, n, :], in_hi[:, n, :].bitcast(F32), ALU.subtract).then_inc(in_lo_done, 1)
            split_lo(J_BS - 7, 0)

            def wo_low(n):
                dve.wait_ge(in_hi_done, 3 * KT + n + 1)
                tt(wo_lo[:, n, :], wo_raw[:, n, :], wo_hi[n].bitcast(F32), ALU.subtract).then_inc(in_lo_done, 1)

            def merge(i, q, last):
                n = 2 * i + q
                if last:
                    for t in range(3):
                        wo_low(t)
                dve.wait_ge(g_in[q], 16 * i + 16)
                dve.wait_ge(mm_done, J_BS + n + 1)
                stt(gt[q][:, :], gt[q][:, :], 1.0, ps[q][:, :], ALU.add, ALU.mult).then_inc(job_out[q], 1)
                dve.wait_ge(job_out[q], half(J_BS, 2, i, q) + 1)
                dve.wait_ge(reload_in[q], 16 * i + 16 * 5)
                tt(rt[q][:, :], gt[q][:, :], rt[q][:, :], ALU.add).then_inc(m_sum, 1)
                if last:
                    for t in range(3, 7):
                        wo_low(t)
                dve.wait_ge(m_hi_done, n + 1)
                tt(m_lo[:, n, :], rt[q][:, :], m_hi[:, n, :].bitcast(F32), ALU.subtract).then_inc(m_lo_done, 1)

            def turn4(i, last):
                for q in range(2):
                    if not (last and q == 1):
                        split_lo(2 * i + J_BS + q + 1 - 7, (q + 1) % 2)
                    merge(i, q, last and q == 1)

            with dve.Fori(0, 3) as i:
                turn4(i, False)
            turn4(3, True)
            wo_low(KT - 1)
            dve.wait_ge(row_ready, 1)
            for t in range(CH):
                one = slice(t, t + 1)
                last = t == CH - 1
                dve.wait_ge(o_sums, t + 1 + last)
                if last:
                    do(tt(stat[:, 0, one], stat[:, 0, one], stat[:, 5, one], ALU.add))
                ts(stat[:, 1, one], stat[:, 0, one], 0.25 / D, EPS, ALU.mult, ALU.add).then_inc(o_var, 1)
                dve.wait_ge(o_root, t + 1)
                newton(steps, one, 0.5)
                if t >= 2:
                    dve.wait_ge(out_stored[t % 2], 16 * (t // 2))
                parts = [slice(0, HALF), slice(HALF, D)] if last else [slice(0, D)]
                for n, part in enumerate(parts):
                    stt(gt[t % 2][:, part], ps[t % 2][:, part], stat[:, 4, one], gate_row[:, part],
                        ALU.mult, ALU.mult).then_inc(job_out[t % 2], 1)
                    dve.wait_ge(job_out[t % 2], (J_OUT + t) // 2 + 1 + n)
                    dve.wait_ge(reload_in[t % 2], 16 * (9 + t // 2))
                    tt(gt[t % 2][:, part], gt[t % 2][:, part], rt[t % 2][:, part], ALU.add).then_inc(o_ready, 1)

        @block.tensor
        def _(pe):
            mm = nc.tensor.matmul
            pe.sem_inc(a_done, 1)
            pe.sem_inc(y_done, 1)

            def product(nth, before, slot, x_hi, x_lo, arrives=None, transposed=False):
                pe.wait_ge(hi_done, nth)
                if before is not None:
                    pe.wait_ge(job_out[slot], before)
                for k in range(KT):
                    if transposed and k < KT - 3:
                        x_transposed(k + 3)
                    if arrives:
                        pe.wait_ge(arrives[0], arrives[1] + k + 1)
                    for q, (a, b) in enumerate(((w_hi, x_hi), (w_hi, x_lo), (w_lo, x_hi))):
                        for f in range(2):
                            last = mm(ps[slot][:, f * HALF:f * HALF + HALF], a[slot][:, k, :],
                                      b[:, k, f * HALF:f * HALF + HALF],
                                      start=k == 0 and q == 0, stop=k == KT - 1 and q == 2)
                last.then_inc(mm_done, 1)

            def plain(j, w, xs, arrives=None, transposed=False):
                pe.wait_ge(raw_free[w % 2], w // 2 + 1)
                product(j + 1 if j < J_P else j - 7, j // 2 or None, j % 2, *xs, arrives=arrives, transposed=transposed)

            h = (h_hi, h_lo)

            def x_transposed(k):
                if k >= 3:
                    pe.wait_ge(h_full, k - 2)
                for t in range(CH):
                    last = mm(xt[k % 3][:, t * P:t * P + P], x_tok[:, t, k * P:k * P + P], diag[:, t, :],
                              start=True, stop=True)
                last.then_inc(xt_done, 1)

            pe.wait_ge(x_scaled, CH)
            for k in range(3):
                x_transposed(k)
            for w in range(5):
                if w == 0:
                    plain(J_G, 0, h, (h_done, 0), transposed=True)
                else:
                    plain(J_G + w, w, h)

            def part_a1(b):
                pe.wait_ge(v_ready, b + 1)
                pe.wait_ge(x_taken, b + 1)
                for g in range(GB):
                    vg = v[:, g, :, :].rearrange("p j h -> p (j h)")
                    last = nc.tensor.transpose(psa[:, g * P:g * P + P], vg, ident)
                last.then_inc(turned, 1)

            def part_a2(b):
                pe.wait_ge(y_taken, b + 1)
                for g in range(GB):
                    vg = v[:, g, :, :].rearrange("p j h -> p (j h)")
                    last = mm(psb[:, g * SG:g * SG + SG], vg, cc[:, g, :], start=True, stop=True)
                last.then_inc(a_done, 1)

            def part_b(b):
                pe.wait_ge(win_ready, b + 1)
                pe.wait_ge(u_loaded, 16 * CH * b + 16 * CH)
                for g in range(GB):
                    last = mm(psa[:, g * P:g * P + P], win[:, g, :], u_in[:, g, :], start=True, stop=True)
                last.then_inc(x_done, 1)

            def part_c(b):
                pe.wait_ge(sq_ready, b + 1)
                pe.wait_ge(wout_ready, b + 1)
                pe.wait_ge(k_taken, b + 1)
                pe.wait_ge(taps_ready, b + 1)
                for g in range(GB):
                    mm(psb[:, g * P:g * P + P], taps[:, g, :, :].rearrange("p r h -> p (r h)"), u_in[:, g, :], start=True, stop=False)
                    last = mm(psb[:, g * P:g * P + P], wout[:, g, :, :].rearrange("p r h -> p (r h)"), sq[:, g, :],
                              start=False, stop=True)
                last.then_inc(y_done, 1)

            part_a1(0)

            def turn1(i, last):
                def job(k):
                    pe.wait_ge(raw_free[(W_P + k) % 2], half(W_P, 6, i, k) + 1)
                    product(W_P + 6 * i + k + 1, half(J_P, 8, i, k), (J_P + k) % 2, *h)

                def pool_product(q):
                    slot = 1 - q
                    pe.wait_ge(job_out[slot], half(J_P, 8, i, 6 + q))
                    for k in range(2):
                        for p, (a, b) in enumerate(((pw_hi, pool_hi), (pw_hi, pool_lo), (pw_lo, pool_hi))):
                            for f in range(2):
                                last_ = mm(ps[slot][:, f * HALF:f * HALF + HALF], a[:, 2 * q + k, :],
                                           b[:, k, f * HALF:f * HALF + HALF],
                                           start=k == 0 and p == 0, stop=k == 1 and p == 2)
                    last_.then_inc(mm_done, 1)

                n = 2 * i
                job(0)
                part_a2(n)
                part_b(n)
                job(1)
                job(2)
                part_c(n)
                part_a1(n + 1)
                job(3)
                part_a2(n + 1)
                part_b(n + 1)
                job(4)
                job(5)
                part_c(n + 1)
                if not last:
                    part_a1(n + 2)
                pe.wait_ge(pw_ready, i + 1)
                pe.wait_ge(pool_lo_done, n + 2)
                for q in range(2):
                    pool_product(q)

            with pe.Fori(0, 3) as i:
                turn1(i, False)
            turn1(3, True)

            plain(J_F1, W_F1, h)
            with pe.Fori(0, 4) as i:
                def job2(k, w, xs):
                    pe.wait_ge(raw_free[k % 2], half(W_BP, 6, i, w) + 1)
                    product(4 * i + J_BP + k - 7, half(J_BP, 4, i, k), k % 2, *xs,
                            arrives=(in_lo_done, 0) if k == 1 else None)

                job2(0, 0, h)
                job2(1, 1, (in_hi, in_lo))
                job2(2, 2, h)
                job2(3, 5, (in_hi, in_lo))
            with pe.Fori(0, 4) as i:
                for k in range(4):
                    pe.wait_ge(raw_free[k % 2], half(W_GLU, 4, i, k) + 1)
                    product(4 * i + J_GLU + k - 7, half(J_GLU, 4, i, k), k % 2, *(h if k % 2 == 0 else (in_hi, in_lo)),
                            arrives=(in_lo_done, KT) if k == 1 else None)
            plain(J_F3, W_F3, h)
            pe.wait_ge(diag_ready, KT + 1)
            for f in range(2):
                last = mm(psa[:, f * HALF:f * HALF + HALF], ones[:, :], gate_row[:, f * HALF:f * HALF + HALF],
                          start=True, stop=True)
            last.then_inc(row_done, 1)
            plain(J_F3 + 1, W_F3 + 1, h)
            with pe.Fori(0, 4) as i:
                for k in range(2):
                    pe.wait_ge(raw_free[k % 2], half(W_BS, 2, i, k) + 1)
                    product(2 * i + J_BS + k - 7, half(J_BS, 2, i, k), k % 2, in_hi, ys_lo,
                            arrives=(in_lo_done, 2 * KT) if k == 0 else None)
            def out_tile(t, k, f, first, final):
                for q, (a, b) in enumerate(((m_hi, wo_hi[k]), (m_hi, wo_lo[:, k, :]), (m_lo, wo_hi[k]))):
                    ins = mm(ps[t % 2][:, f * HALF:f * HALF + HALF], a[:, k, t * P:t * P + P],
                             b[:, f * HALF:f * HALF + HALF], start=first and q == 0, stop=final and q == 2)
                return ins

            for t in range(CH):
                pe.wait_ge(job_out[t % 2], (J_OUT + t) // 2)
                if t < CH - 1:
                    for k in range(KT):
                        if t == 0:
                            pe.wait_ge(m_lo_done, k + 1)
                            pe.wait_ge(in_lo_done, 3 * KT + k + 1)
                        for f in range(2):
                            ins = out_tile(t, k, f, k == 0, k == KT - 1)
                    ins.then_inc(mm_done, 1)
                else:
                    for f in range(2):
                        for k in range(KT):
                            ins = out_tile(t, k, f, k == 0, k == KT - 1)
                        ins.then_inc(mm_done, 1)


def kernel(x, c, w_ada, b_ada, norm_pre, norm_post, w_in, pool_w, pool_scale,
           ssm_a_re, ssm_a_im, ssm_log_dt, ssm_b_re, ssm_b_im, ssm_c_re, ssm_c_im,
           ssm_d, glu_w, glu_b, w_branch_pool, w_branch_ssm, w_out):
    import numpy as np
    import concourse.bacc as bacc
    from concourse.bass_utils import run_bass_kernel_spmd

    def column(vec):
        return np.asarray(vec).reshape(-1, P).T

    def tiles(w):
        w = np.asarray(w)
        return w.reshape(w.shape[0] // P, P, w.shape[1] // P, P).transpose(2, 1, 0, 3)

    ada = np.asarray(w_ada[0]).T.reshape(3 * KT, P, D)
    win = tiles(w_in[0])
    u_pool, z_pool, u_ssm, z_ssm, g_pool, g_ssm = (win[KT * q:KT * q + KT] for q in range(6))
    pw = np.asarray(pool_w[0])
    pool = pw.reshape(4, 2, P, 2, P).transpose(0, 2, 3, 1, 4).reshape(4, P, 4, P)
    wbp, wbs, glu = tiles(w_branch_pool[0]), tiles(w_branch_ssm[0]), tiles(glu_w[0])
    gate = ada[2 * KT:].reshape(KT, P, KT, P)
    stream = [g_ssm[n] for n in range(4)] + [u_ssm[0]]
    for i in range(4):
        a, b = 2 * i, 2 * i + 1
        stream += [u_pool[a], z_pool[a], u_ssm[b], u_pool[b], z_pool[b], u_ssm[b + 1] if i < 3 else g_ssm[4]]
    stream += [g_ssm[5]]
    for i in range(4):
        a, b = 2 * i, 2 * i + 1
        stream += [g_pool[a], wbp[a], g_pool[b], gate[a], gate[b], wbp[b]]
    for i in range(4):
        a, b = 2 * i, 2 * i + 1
        stream += [z_ssm[a], glu[a], z_ssm[b], glu[b]]
    stream += [g_ssm[6], g_ssm[7]] + [wbs[n] for n in range(KT)]

    cols = np.concatenate([column(v) for v in (norm_pre[0], b_ada[0], norm_post[0], pool_scale[0],
                                               glu_b[0])], 1)
    consts = np.zeros((P, 232), np.float32)
    consts[:, 0:128] = np.eye(P)
    consts[:, 128] = np.where(np.arange(P) < NS, 1.0, -1.0)
    for q, w in enumerate(WINDOWS):
        consts[:, 129 + 4 * q:133 + 4 * q] = [1.0 if (2 << l) <= w else 0.0 for l in range(LEVELS)]
        consts[:, 145 + q] = 1.0 / w
        for t in range(CH):
            for ch in range(2):
                consts[:, 149 + 16 * q + 2 * t + ch] = 1.0 / min(w, 8 * ch + t + 1)
    for h in range(SG):
        consts[P - SG + h, 213 + h] = 1.0

    def stack(top, low):
        return np.concatenate([np.moveaxis(np.asarray(top), 1, 0), np.moveaxis(np.asarray(low), 1, 0)], 0)

    b_re, b_im = np.asarray(ssm_b_re[0]), np.asarray(ssm_b_im[0])
    c_re, c_im = (np.swapaxes(np.asarray(m[0]), 1, 2) for m in (ssm_c_re, ssm_c_im))
    d_all = np.broadcast_to(np.asarray(ssm_d[0]), (P, G, SG))
    bcs = np.stack([stack(b_re, b_im), stack(b_im, b_re), stack(c_re, c_im), stack(c_im, c_re), d_all], 1)
    bcs = bcs.reshape(P, 5, KT, GB * SG).transpose(2, 0, 1, 3).reshape(KT, P, 5 * GB * SG)
    arrays = {
        "x": x, "c": np.broadcast_to(np.asarray(c[0]), (P, D)), "cols": cols, "consts": consts,
        "a_re": stack(ssm_a_re[0], ssm_a_re[0]), "a_im": stack(ssm_a_im[0], ssm_a_im[0]),
        "log_dt": np.broadcast_to(np.asarray(ssm_log_dt[0]), (P, G)),
        "bc": bcs, "w_ada": ada[0:2 * KT], "wstream": np.stack(stream), "pool": pool, "w_out": w_out[0],
    }
    arrays = {f"in_{k}": np.ascontiguousarray(a) for k, a in arrays.items()}
    nc = bacc.Bacc("TRN2", target_bir_lowering=False, num_devices=1)
    args = [nc.dram_tensor(k, a.shape, mybir.dt.from_np(a.dtype), kind="ExternalInput").ap()
            for k, a in arrays.items()]
    args.append(nc.dram_tensor("out", (1, SEQ, D), F32, kind="ExternalOutput").ap())
    build(nc, *args)
    r = run_bass_kernel_spmd(nc, [arrays], core_ids=[0])
    return r.results[0]["out"]
```
